# Optimizing a Trainium2 kernel written in Bass

```python
import jax, jax.numpy as jnp
from jax import lax
import numpy as np

D_MODEL = 1024
BATCH = 1
SEQ = 1024
DEPTH = 1

MIX_WIDTH = D_MODEL
C_CONV = MIX_WIDTH // 2
CONV_HEADS = 8
C_POOL = MIX_WIDTH - C_CONV
POOL_WINDOWS = (2, 4, 8, 16)
N_POOL_GROUPS = len(POOL_WINDOWS)
POOL_GROUP = C_POOL // N_POOL_GROUPS
CONV_K = 31
D_FF = ((8 * D_MODEL // 3 + 255) // 256) * 256
D_PLE = 256
EPS = 1e-6

kernel_name = "hybrid_conformer_conv_multiscale_pool_block"

def rmsnorm(x, g):
    xf = x.astype(jnp.float32)
    y = xf * lax.rsqrt(jnp.mean(xf * xf, axis=-1, keepdims=True) + EPS)
    return (y * g.astype(jnp.float32)).astype(x.dtype)

def layernorm(x, g, b):
    xf = x.astype(jnp.float32)
    mu = jnp.mean(xf, axis=-1, keepdims=True)
    var = jnp.mean(jnp.square(xf - mu), axis=-1, keepdims=True)
    y = (xf - mu) * lax.rsqrt(var + EPS)
    return (y * g.astype(jnp.float32) + b.astype(jnp.float32)).astype(x.dtype)

def causal_depthwise_conv(u, w, b):
    c = u.shape[-1]
    k = w.reshape(CONV_K, 1, c).astype(u.dtype)
    y = lax.conv_general_dilated(
        u, k, window_strides=(1,), padding=[(CONV_K - 1, 0)],
        dimension_numbers=("NWC", "WIO", "NWC"), feature_group_count=c)
    return y + b.astype(u.dtype)

def multiscale_pool(v, pool_w, pool_scale):
    s = v.shape[1]
    vf = v.astype(jnp.float32)
    groups = vf.reshape(vf.shape[0], s, N_POOL_GROUPS, POOL_GROUP)
    pos1 = jnp.arange(1, s + 1, dtype=jnp.float32)[None, :, None]
    outs = []
    for g, w in enumerate(POOL_WINDOWS):
        vg = groups[:, :, g, :]
        c = jnp.cumsum(vg, axis=1)
        c_shift = jnp.pad(c, ((0, 0), (w, 0), (0, 0)))[:, :s]
        cnt = jnp.minimum(pos1, float(w))
        outs.append((c - c_shift) / cnt - vg)
    pooled = jnp.stack(outs, axis=2)
    mixed = jnp.einsum("bsgc,gcd->bsgd", pooled, pool_w.astype(jnp.float32))
    mixed = mixed.reshape(vf.shape) * pool_scale.astype(jnp.float32)
    return mixed.astype(v.dtype)

def setup_inputs(seed: int = 0) -> dict:
    key = jax.random.key(seed)
    ks = jax.random.split(key, 20)
    L, D = DEPTH, D_MODEL
    n = lambda k, shape, fan: jax.random.normal(k, shape, jnp.float32) * (fan ** -0.5)
    gain = lambda k, shape: 1.0 + 0.05 * jax.random.normal(k, shape, jnp.float32)
    return {
        "x": jax.random.normal(ks[0], (BATCH, SEQ, D), jnp.float32),
        "p": jax.random.normal(ks[1], (DEPTH, BATCH, SEQ, D_PLE), jnp.float32),
        "g_mix": gain(ks[2], (L, D)),
        "w_in": n(ks[3], (L, D, 2 * C_CONV + C_POOL), D),
        "conv_w": n(ks[4], (L, CONV_K, C_CONV), CONV_K),
        "conv_b": 0.02 * jax.random.normal(ks[5], (L, C_CONV), jnp.float32),
        "ln_g": gain(ks[6], (L, C_CONV)),
        "ln_b": 0.02 * jax.random.normal(ks[7], (L, C_CONV), jnp.float32),
        "pool_w": n(ks[8], (L, N_POOL_GROUPS, POOL_GROUP, POOL_GROUP), POOL_GROUP),
        "pool_scale": gain(ks[9], (L, C_POOL)),
        "w_out": n(ks[10], (L, MIX_WIDTH, D), MIX_WIDTH),
        "g_ffn": gain(ks[11], (L, D)),
        "w_gate_up": n(ks[12], (L, D, 2 * D_FF), D),
        "w_down": n(ks[13], (L, D_FF, D), D_FF),
        "g_ple_gate": gain(ks[14], (L, D)),
        "w_ple_gate": n(ks[15], (L, D, D), D),
        "w_ple_up": n(ks[16], (L, D_PLE, D), D_PLE),
        "g_ple_post": gain(ks[17], (L, D)),
        "g_final": gain(ks[18], (D,)),
    }

def reference(x, p, g_mix, w_in, conv_w, conv_b, ln_g, ln_b, pool_w, pool_scale,
              w_out, g_ffn, w_gate_up, w_down, g_ple_gate, w_ple_gate, w_ple_up,
              g_ple_post, g_final):
    for i in range(DEPTH):
        h = rmsnorm(x, g_mix[i])
        z = h @ w_in[i]
        a = z[..., :C_CONV]
        b = z[..., C_CONV:2 * C_CONV]
        v = z[..., 2 * C_CONV:]
        u = a * jax.nn.sigmoid(b)
        u = causal_depthwise_conv(u, conv_w[i], conv_b[i])
        u = jax.nn.silu(layernorm(u, ln_g[i], ln_b[i]))
        q = multiscale_pool(v, pool_w[i], pool_scale[i])
        mix = jnp.concatenate([u, q], axis=-1)
        x = x + mix @ w_out[i]
        h = rmsnorm(x, g_ffn[i])
        gu = h @ w_gate_up[i]
        x = x + (jax.nn.silu(gu[..., :D_FF]) * gu[..., D_FF:]) @ w_down[i]
        gate = jax.nn.sigmoid(rmsnorm(x, g_ple_gate[i]) @ w_ple_gate[i])
        e = rmsnorm(p[i].astype(x.dtype) @ w_ple_up[i], g_ple_post[i])
        x = x + gate * e
    return rmsnorm(x, g_final)


_drawn_inputs = setup_inputs


def setup_inputs(seed=0):
    import zlib

    import numpy as np

    out = dict(_drawn_inputs(seed))
    spreads = {}
    factors = {'conv_b': 3.937, 'ln_b': 8.0, 'g_ple_gate': 8.0, 'g_ple_post': 3.139}
    for name, (base, spread) in spreads.items():
        noise = np.random.default_rng([zlib.crc32(name.encode()), seed]).standard_normal(out[name].shape)
        drawn = base * np.exp(spread * noise) if base else spread * noise
        out[name] = __import__('jax').numpy.asarray(drawn.astype(out[name].dtype))
    for name, factor in factors.items():
        out[name] = (out[name] * factor).astype(out[name].dtype)
    return out
```

```python
from contextlib import ExitStack

import numpy as np

import concourse.bass as bass
from concourse import mybir

F32, F32R, BF16 = mybir.dt.float32, mybir.dt.float32r, mybir.dt.bfloat16
ALU, ACT = mybir.AluOpType, mybir.ActivationFunctionType

P = 128
EPS = 1e-6
BANK = 512
HEADPAD = 16
DMA = 16


def hybrid_block(nc, x, p, g_mix, w_in, conv_w, conv_b, ln_g, ln_b, pool_w, pool_scale, w_out,
                 g_ffn, w_gate_up, w_down, g_ple_gate, w_ple_gate, w_ple_up, g_ple_post,
                 g_final, out):
    SEQ, D = x.shape[1], x.shape[2]
    C = conv_w.shape[2]
    TAPS = conv_w.shape[1]
    GROUPS = pool_w.shape[1]
    F = w_down.shape[1]
    DP = p.shape[3]
    TT = SEQ // P
    KD = D // P
    KC = C // P
    KP = DP // P
    HALVES = SEQ // BANK
    HT = TT // HALVES
    NCH = F // (2 * P)
    PAD = TAPS - 1
    UW = PAD + SEQ
    assert (SEQ, D, C, KD, KC, KP, GROUPS, HALVES) == (1024, 1024, 512, 8, 4, 2, 4, 2)
    assert F == NCH * 2 * P

    x_v = x[0].rearrange("(t p) d -> t p d", p=P)
    out_v = out[0].rearrange("(t p) d -> t p d", p=P)
    p_v = p[0, 0].rearrange("(t p) d -> p t d", p=P)
    w_in_v = w_in[0].rearrange("(k p) n -> p k n", p=P)
    w_gu_v = w_gate_up[0].rearrange("(k p) n -> p k n", p=P)
    w_out_v = w_out[0].rearrange("(k p) n -> p k n", p=P)
    w_dn_v = w_down[0].rearrange("(f p) n -> p f n", p=P)
    w_pg_v = w_ple_gate[0].rearrange("(k p) n -> p k n", p=P)
    w_pu_v = w_ple_up[0].rearrange("(k p) n -> p k n", p=P)
    e_dram = nc.dram_tensor("e_scratch", (TT, P, D), F32, kind="Internal").ap()

    with ExitStack() as ctx:
        def sb(name, shape, dt=F32):
            return ctx.enter_context(nc.sbuf_tensor(name, shape, dt))

        def sem(name):
            return ctx.enter_context(nc.semaphore(name))

        resid = sb("resid", [P, KC * UW + KC * SEQ])
        xres = resid[:, 0:TT * D].rearrange("p (t d) -> p t d", t=TT)
        u_all = resid[:, 0:KC * UW].rearrange("p (c s) -> p c s", c=KC)
        conv_o = resid[:, KC * UW:KC * UW + KC * SEQ].rearrange("p (c s) -> p c s", c=KC)
        act_hi = sb("act_hi", [P, KD, SEQ], F32R)
        act_lo = sb("act_lo", [P, KD, SEQ], F32R)
        ws_hi = sb("ws_hi", [P, 4, 1024], F32R)
        ws_lo = sb("ws_lo", [P, 4, 1024], F32R)
        bs_hi = sb("bs_hi", [P, 4, 1024], F32R)
        bs_lo = sb("bs_lo", [P, 4, 1024], F32R)
        raw = sb("raw", [P, 4, 1024])
        raw_b = sb("raw_b", [P, 2, 1024])
        wide = sb("wide", [P, 4, SEQ + HEADPAD])
        wide_f = wide[:, :, :].rearrange("p a b -> p (a b)")
        scr = sb("scr", [P, 3, 1024])
        gain = sb("gain", [P, D])
        junk = sb("junk", [P, 1024], BF16)
        ident = sb("ident", [P, P])
        convw = sb("convw", [P, KC * 32])
        cvec = sb("cvec", [P, 4 * KC])
        convb, lng, lnb, pscale = (cvec[:, KC * n:KC * (n + 1)] for n in range(4))
        inv_cnt = sb("inv_cnt", [P, HEADPAD])
        neg_half = sb("neg_half", [P, 1])
        ss = sb("ss", [P, 5 * TT])
        rs = sb("rs", [P, 5 * TT])
        bst = sb("bst", [P, TT, 6])
        mv = sb("mv", [P, TT, 2])
        lrs = sb("lrs", [P, TT])
        ps = ctx.enter_context(nc.psum_tensor("ps", [P, 8, BANK], F32))

        def cols_of(w, m):
            piece = w[:, 2 * (m % 2):2 * (m % 2) + 2, :].rearrange("p a (b n) -> p (a b) n", n=2 * P)
            return piece[:, :, (m // 2) * P:(m // 2 + 1) * P]

        def pair(b):
            return ps[:, b:b + 2, :].rearrange("p a b -> p (a b)")

        x_in = [sem(f"x_in{t}") for t in range(TT)]
        const_in = sem("const_in")
        gain_in = sem("gain_in")
        raw_in = [sem(f"raw_in{j}") for j in range(2)]
        rawb_in = sem("rawb_in")
        e_stored = [sem(f"e_stored{j}") for j in range(2)]
        e_in = [sem(f"e_in{j}") for j in range(2)]
        gfin_in = sem("gfin_in")
        out_stored = [sem(f"out_stored{j}") for j in range(2)]
        ident_ok = sem("ident_ok")
        tables_ok = sem("tables_ok")
        upad_ok = sem("upad_ok")
        ss_ok = sem("ss_ok")
        ms_ok = sem("ms_ok")
        rs_ok = sem("rs_ok")
        xn_ok = sem("xn_ok")
        turned = sem("turned")
        act_hi_ok = sem("act_hi_ok")
        act_lo_ok = sem("act_lo_ok")
        w_hi = sem("w_hi")
        w_lo = sem("w_lo")
        wd_hi = sem("wd_hi")
        wd_lo = sem("wd_lo")
        ab_mm = sem("ab_mm")
        ab_ev = sem("ab_ev")
        u_ok = sem("u_ok")
        taps_done = sem("taps_done")
        v_mm = sem("v_mm")
        v_ev = sem("v_ev")
        win_step = sem("win_step")
        win_ok = sem("win_ok")
        mean_ok = sem("mean_ok")
        head_ok = sem("head_ok")
        pooled_ok = sem("pooled_ok")
        pooled_hi = sem("pooled_hi")
        pooled_lo = sem("pooled_lo")
        pw_hi_ok = sem("pw_hi_ok")
        pw_lo_ok = sem("pw_lo_ok")
        p_turned = sem("p_turned")
        p_copied = sem("p_copied")
        p_lo_ok = sem("p_lo_ok")
        e_mm = sem("e_mm")
        e_ss = sem("e_ss")
        e_ms = sem("e_ms")
        e_rs = sem("e_rs")
        e_ok = sem("e_ok")
        q_mm = sem("q_mm")
        q_copied = sem("q_copied")
        q_lo_ok = sem("q_lo_ok")
        lnf_mm = sem("lnf_mm")
        bn_ok = sem("bn_ok")
        mv_ok = sem("mv_ok")
        var_ok = sem("var_ok")
        lrs_ok = sem("lrs_ok")
        n_ok = sem("n_ok")
        lnb_mm = sem("lnb_mm")
        y_ok = sem("y_ok")
        silu_ok = sem("silu_ok")
        mix_hi_ok = sem("mix_hi_ok")
        mix_lo_ok = sem("mix_lo_ok")
        const_mm = sem("const_mm")
        const_ok = sem("const_ok")
        rows_done = sem("rows_done")
        rows_added = sem("rows_added")
        gu_mm = sem("gu_mm")
        sig_ok = sem("sig_ok")
        gs_ok = sem("gs_ok")
        in_ok = sem("in_ok")
        in_hi = sem("in_hi")
        in_lo = sem("in_lo")
        pg_hi = sem("pg_hi")
        pg_lo = sem("pg_lo")
        pg_mm = sem("pg_mm")
        gate_ok = sem("gate_ok")
        eg_ok = sem("eg_ok")
        ge_ok = sem("ge_ok")
        res_ok = sem("res_ok")
        fin_ok = sem("fin_ok")

        N_IN, N_PLE, N_WO = 12, KP, KD
        GU0 = N_IN + N_PLE + N_WO
        TURN_BANK = (6, 6, 0)

        block = ctx.enter_context(nc.Block())

        @block.sync
        def _(sp):
            def load_gain(g, wait=None):
                sp.dma_start(gain[:, :], g.partition_broadcast(P)).then_inc(gain_in, DMA)

            def load_cols(view, lo, hi):
                for j, first in enumerate((lo, hi)):
                    sp.dma_start(raw[:, 2 * j:2 * j + 2, :].rearrange("p a (b n) -> p (a b) n", n=256),
                                 view[:, :, bass.ds(first, 256)]).then_inc(raw_in[j], DMA)

            def load_rows(j, rows):
                sp.dma_start(raw[:, 2 * j:2 * j + 2, :], rows).then_inc(raw_in[j], DMA)

            def load_x(t, dst):
                sp.dma_start(dst, x_v[t]).then_inc(x_in[t], DMA)

            sp.dma_start(scr[0:TAPS, 2, 0:C], conv_w[0]).then_inc(const_in, DMA)
            for n, src in enumerate((conv_b, ln_g, ln_b, pool_scale)):
                sp.dma_start(scr[KC * n:KC * (n + 1), 2, C:C + P], src[0].rearrange("(c p) -> c p", p=P))\
                  .then_inc(const_in, DMA)
            load_x(0, xres[:, 0, :])
            load_gain(g_mix[0])
            load_x(1, xres[:, 1, :])
            load_cols(w_in_v, 0, C)
            for t in range(2, TT):
                load_x(t, xres[:, t, :])
            sp.dma_start(raw_b[:, :, :].rearrange("p a (t d) -> p (a t) d", d=DP), p_v).then_inc(rawb_in, DMA)
            sp.wait_ge(w_lo, 4)
            load_cols(w_in_v, 256, C + 256)
            sp.wait_ge(xn_ok, TT)
            sp.dma_start(gain[:, 0:GROUPS * P].rearrange("p (g d) -> p g d", g=GROUPS),
                         pool_w[0].rearrange("g c d -> c g d")).then_inc(gain_in, DMA)
            sp.wait_ge(w_lo, 8)
            load_cols(w_in_v, 2 * C, 2 * C + 256)
            sp.wait_ge(w_lo, 12)
            load_rows(0, w_pu_v)
            load_rows(1, w_out_v[:, 6:8, :])
            sp.wait_ge(w_lo, 16)
            load_rows(0, w_out_v[:, 4:6, :])
            load_rows(1, w_out_v[:, 0:2, :])
            for t in range(TT):
                sp.wait_ge(e_ok, t + 1)
                sp.dma_start(e_dram[t], gain[:, :] if t % 2 else scr[:, 0, :]).then_inc(e_stored[t % 2], DMA)
            sp.wait_ge(p_turned, 4)
            load_x(0, raw_b[:, 0, :])
            load_x(1, raw_b[:, 1, :])
            sp.wait_ge(e_stored[1], DMA * (TT // 2))
            sp.wait_ge(e_stored[0], DMA * (TT // 2))
            load_gain(g_ffn[0])
            sp.wait_ge(w_lo, 18)
            load_rows(0, w_out_v[:, 2:4, :])
            sp.wait_ge(w_lo, GU0)
            load_cols(w_gu_v, 0, F)
            for t in range(2, TT):
                sp.wait_ge(rows_added, 2 * (t - 1))
                load_x(t, raw_b[:, t % 2, :])
            sp.wait_ge(rows_added, 2 * TT)
            sp.dma_start(raw_b[:, :, :], w_dn_v[:, 0:2, :]).then_inc(rawb_in, DMA)
            sp.wait_ge(xn_ok, 2 * TT)
            load_gain(g_ple_gate[0])
            with sp.Fori(0, NCH - 1) as i:
                sp.wait_ge(w_lo, i * 4 + (GU0 + 4))
                load_cols(w_gu_v, (i + 1) * 256, (i + 1) * 256 + F)
                sp.wait_ge(wd_lo, i * 2 + 2)
                sp.dma_start(raw_b[:, :, :], w_down[0][bass.ds((i + 1) * 256, 256), :]
                             .rearrange("(f p) n -> p f n", p=P)).then_inc(rawb_in, DMA)
            sp.wait_ge(w_lo, GU0 + 4 * NCH)
            load_rows(0, w_pg_v[:, 0:2, :])
            load_rows(1, w_pg_v[:, 2:4, :])
            for j in range(2):
                sp.dma_start(wide[:, 2 + j, 0:D], e_dram[j]).then_inc(e_in[j], DMA)
            sp.wait_ge(wd_lo, 2 * NCH)
            sp.dma_start(raw_b[:, 0, :], g_ple_post[0].partition_broadcast(P)).then_inc(gfin_in, DMA)
            sp.dma_start(raw_b[:, 1, :], g_final.partition_broadcast(P)).then_inc(gfin_in, DMA)
            sp.wait_ge(w_lo, GU0 + 4 * NCH + 4)
            load_rows(0, w_pg_v[:, 4:6, :])
            load_rows(1, w_pg_v[:, 6:8, :])
            for t in range(TT):
                if t + 2 < TT:
                    sp.wait_ge(ge_ok, t + 1)
                    sp.dma_start(wide[:, 2 + t % 2, 0:D], e_dram[t + 2]).then_inc(e_in[t % 2], DMA)
                sp.wait_ge(fin_ok, t + 1)
                sp.dma_start(out_v[t], scr[:, t % 2, :]).then_inc(out_stored[t % 2], DMA)
            for j in range(2):
                sp.wait_ge(out_stored[j], DMA * (TT // 2))

        @block.gpsimd
        def _(pool):
            def rms(n, ready, ms_done, done, k):
                pool.wait_ge(ready, k)
                pool.tensor_scalar(ss[:, n:n + 1], ss[:, n:n + 1], 1.0 / D, EPS, ALU.mult, ALU.add)\
                    .then_inc(ms_done, 1)
                pool.wait_ge(ms_done, k)
                pool.tensor_tensor(rs[:, n:n + 1], ss[:, n:n + 1], neg_half[:, :], ALU.pow).then_inc(done, 1)

            def lo(dst, src, hi, done):
                pool.tensor_tensor(dst, src, hi.bitcast(F32), ALU.subtract).then_inc(done, 1)

            def split_cols(m, n):
                pool.wait_ge(w_hi, n)
                src, hi = cols_of(raw, m), ws_hi[:, m, :].rearrange("p (k n) -> p k n", k=KD)
                lo(ws_lo[:, m, :].rearrange("p (k n) -> p k n", k=KD), src, hi, w_lo)

            def split_row(r, dst_hi, dst_lo, n):
                pool.wait_ge(w_hi, n)
                lo(dst_lo, raw[:, r, :], dst_hi, w_lo)

            pool.memset(ident[:, :], 0.0).then_inc(ident_ok, 1)
            pool.memset(neg_half[:, :], -0.5).then_inc(tables_ok, 1)
            pool.wait_ge(ident_ok, 1)
            pool.affine_select(out=ident[:, :], in_=ident[:, :], compare_op=ALU.not_equal, fill=1.0,
                               base=0, pattern=[[-1, P]], channel_multiplier=1).then_inc(ident_ok, 1)
            for n in range(HEADPAD):
                pool.memset(inv_cnt[:, n:n + 1], 1.0 / (n + 1)).then_inc(tables_ok, 1)
            pool.memset(wide[:, :, 0:HEADPAD], 0.0).then_inc(tables_ok, 1)
            pool.wait_ge(tables_ok, HEADPAD + 2)
            for t in range(TT):
                rms(t, ss_ok, ms_ok, rs_ok, t + 1)
                if t in (1, 2):
                    for m in (2 * t - 2, 2 * t - 1):
                        split_cols(m, m + 1)
            pool.wait_ge(xn_ok, TT)
            pool.memset(u_all[:, :, 0:PAD], 0.0).then_inc(upad_ok, 1)

            def gate_u(c):
                for h in range(HALVES):
                    pool.wait_ge(ab_ev, HALVES * c + h + 1)
                    u = u_all[:, c, PAD + h * BANK:PAD + (h + 1) * BANK]
                    pool.tensor_tensor(u, u, scr[:, 0, h * BANK:(h + 1) * BANK], ALU.mult).then_inc(u_ok, 1)

            gate_u(0)
            for m in range(2):
                split_cols(m, 4 + m + 1)
            gate_u(1)
            for m in range(2, 4):
                split_cols(m, 4 + m + 1)
            gate_u(2)
            for m in range(2):
                split_cols(m, 8 + m + 1)
            gate_u(3)
            for m in range(2, 4):
                split_cols(m, 8 + m + 1)
            steps = 0
            for s, g in enumerate((0, 2, 1, 3)):
                v = wide[:, 3 * (s % 2), :]
                pool.wait_ge(v_ev, s + 1)
                src = v
                for j in range(g + 1):
                    dst, sh = wide[:, 1 + j % 2, :], 1 << j
                    if j:
                        pool.wait_ge(win_step, steps)
                    steps += 1
                    ins = pool.tensor_tensor(dst[:, HEADPAD:], src[:, HEADPAD:],
                                             src[:, HEADPAD - sh:HEADPAD + SEQ - sh], ALU.add)
                    ins.then_inc(win_step, 1)
                    src = dst
                pool.wait_ge(mean_ok, s + 1)
                w = 2 << g
                pool.tensor_tensor(scr[:, 1, 0:w], src[:, HEADPAD:HEADPAD + w], inv_cnt[:, 0:w],
                                   ALU.mult).then_inc(head_ok, 1)
                pool.wait_ge(head_ok, s + 1)
                pool.tensor_tensor(scr[:, 1, :], scr[:, 1, :], v[:, HEADPAD:], ALU.subtract).then_inc(pooled_ok, 1)
                pool.wait_ge(pooled_hi, s + 1)
                lo(bs_lo[:, g, :], scr[:, 1, :], bs_hi[:, g, :], pooled_lo)
            for r in range(4):
                split_row(r, ws_hi[:, r, :], ws_lo[:, r, :], N_IN + r + 1)
            pool.wait_ge(pw_hi_ok, 1)
            lo(act_lo[:, 2, 0:GROUPS * P], gain[:, 0:GROUPS * P], act_hi[:, 2, 0:GROUPS * P], pw_lo_ok)
            for k in range(KP):
                pool.wait_ge(p_copied, 2 * (k + 1))
                lo(act_lo[:, k, :], scr[:, 2, :], act_hi[:, k, :], p_lo_ok)
            for t in range(TT):
                rms(4 * TT + t, e_ss, e_ms, e_rs, t + 1)
            for r in range(2):
                split_row(r, ws_hi[:, r, :], ws_lo[:, r, :], N_IN + 4 + r + 1)
            for g in range(GROUPS):
                pool.wait_ge(q_copied, 2 * (g + 1))
                lo(act_lo[:, KC + g, :], scr[:, 2, :], act_hi[:, KC + g, :], q_lo_ok)
            for k in range(4):
                split_row((2, 3, 0, 1)[k], bs_hi[:, k, :], bs_lo[:, k, :], N_IN + 6 + k + 1)
            for t in range(TT):
                pool.wait_ge(var_ok, t + 1)
                pool.tensor_tensor(lrs[:, t:t + 1], mv[:, t, 1:2], neg_half[:, :], ALU.pow).then_inc(lrs_ok, 1)
            for t in range(TT):
                rms(TT + t, ss_ok, ms_ok, rs_ok, TT + t + 1)
            for m in range(4):
                split_cols(m, GU0 + m + 1)

            def ffn_splits(i, last):
                for f in range(2):
                    pool.wait_ge(wd_hi, i * 2 + (f + 1))
                    lo(bs_lo[:, f, :], raw_b[:, f, :], bs_hi[:, f, :], wd_lo)
                for m in range(4):
                    if last:
                        split_row(m, ws_hi[:, m, :], ws_lo[:, m, :], GU0 + 4 * NCH + m + 1)
                    else:
                        split_cols(m, i * 4 + (GU0 + 4 + m + 1))

            with pool.Fori(0, NCH - 1) as i:
                ffn_splits(i, False)
            ffn_splits(NCH - 1, True)

            def times_post(t):
                pool.wait_ge(e_in[t % 2], DMA * (t // 2 + 1))
                if t == 0:
                    pool.wait_ge(gfin_in, 2 * DMA)
                e = wide[:, 2 + t % 2, 0:D]
                pool.tensor_tensor(e, e, raw_b[:, 0, :], ALU.mult).then_inc(eg_ok, 1)

            for t in range(TT):
                rms(2 * TT + t, ss_ok, ms_ok, rs_ok, 2 * TT + t + 1)
                if t < 2:
                    times_post(t)
            for t in range(TT):
                rms(3 * TT + t, ss_ok, ms_ok, rs_ok, 3 * TT + t + 1)
                if t + 2 < TT:
                    times_post(t + 2)

        @block.scalar
        def _(act):
            def copy(dst, src, done, scale=1.0):
                act.activation(dst, src, ACT.Copy, scale=scale).then_inc(done, 1)

            def split_cols(m, raw_count):
                act.wait_ge(raw_in[m % 2], raw_count)
                copy(ws_hi[:, m, :].rearrange("p (k n) -> p k n", k=KD), cols_of(raw, m), w_hi)

            def split_row(r, dst, raw_count):
                act.wait_ge(raw_in[r // 2], raw_count)
                copy(dst, raw[:, r, :], w_hi)

            def square(t, norm):
                act.activation(junk[:, :], xres[:, t, :], ACT.Square,
                               accum_out=ss[:, norm * TT + t:norm * TT + t + 1]).then_inc(ss_ok, 1)

            def turned_hi(t, norm):
                n = norm * TT + t
                for j in range(2):
                    act.wait_ge(turned, 2 * n + j + 1)
                    copy(act_hi[:, 4 * j:4 * j + 4, t * P:(t + 1) * P],
                         ps[:, TURN_BANK[norm] + j, :].rearrange("p (k s) -> p k s", k=4), act_hi_ok)

            for t in range(TT):
                act.wait_ge(x_in[t], DMA)
                if t:
                    act.wait_ge(ss_ok, t)
                square(t, 0)
                if t:
                    turned_hi(t - 1, 0)
                if t in (0, 1):
                    for m in (2 * t, 2 * t + 1):
                        split_cols(m, DMA)
            turned_hi(TT - 1, 0)

            def evac_ab(c):
                for h in range(HALVES):
                    n = HALVES * c + h
                    act.wait_ge(ab_mm, n + 1)
                    if n == 0:
                        act.wait_ge(upad_ok, 1)
                    if c:
                        act.wait_ge(u_ok, n - 1)
                    act.activation(u_all[:, c, PAD + h * BANK:PAD + (h + 1) * BANK], ps[:, 2 * h, :], ACT.Copy)
                    act.activation(scr[:, 0, h * BANK:(h + 1) * BANK], ps[:, 2 * h + 1, :], ACT.Sigmoid)\
                        .then_inc(ab_ev, 1)

            for c in range(KC):
                evac_ab(c)
                act.wait_ge(ab_mm, HALVES * (c + 1))
                for m in (2 * (c % 2), 2 * (c % 2) + 1):
                    split_cols(m, DMA * (2 + c // 2))

            GROUP_AT = (0, 2, 1, 3)

            def evac_v(s):
                act.wait_ge(v_mm, s + 1)
                if s >= 2:
                    act.wait_ge(pooled_ok, s - 1)
                copy(wide[:, 3 * (s % 2), HEADPAD:], pair(2 * (s % 2)), v_ev)

            def means(s):
                g = GROUP_AT[s]
                act.wait_ge(win_step, sum(GROUP_AT[j] + 1 for j in range(s + 1)))
                if s:
                    act.wait_ge(pooled_lo, s)
                copy(scr[:, 1, :], wide[:, 1 + g % 2, HEADPAD:], mean_ok, scale=1.0 / (2 << g))
                act.wait_ge(pooled_ok, s + 1)
                copy(bs_hi[:, g, :], scr[:, 1, :], pooled_hi)

            evac_v(0)
            evac_v(1)
            means(0)
            evac_v(2)
            means(1)
            evac_v(3)
            means(2)
            for k in range(KP):
                act.wait_ge(p_turned, 2 * (k + 1))
                if k:
                    act.wait_ge(p_lo_ok, k)
                act.activation(scr[:, 2, :], pair(2 * k), ACT.Copy).then_inc(p_copied, 1)
                copy(act_hi[:, k, :], pair(2 * k), p_copied)
                if k == 0:
                    means(3)
                    act.wait_ge(v_mm, 2)
                    for r in range(2):
                        split_row(r, ws_hi[:, r, :], 4 * DMA)
                    act.wait_ge(v_mm, 4)
                    for r in range(2, 4):
                        split_row(r, ws_hi[:, r, :], 4 * DMA)
                    act.wait_ge(gain_in, 2 * DMA)
                    copy(act_hi[:, 2, 0:GROUPS * P], gain[:, 0:GROUPS * P], pw_hi_ok)
            def e_square(t):
                act.wait_ge(e_mm, t + 1)
                if t:
                    act.wait_ge(e_ss, t)
                act.activation(junk[:, :], pair(2 * (t % 2)), ACT.Square,
                               accum_out=ss[:, 4 * TT + t:4 * TT + t + 1]).then_inc(e_ss, 1)

            def e_scale(t):
                act.wait_ge(e_rs, t + 1)
                if t >= 2:
                    act.wait_ge(e_stored[t % 2], DMA * (t // 2))
                if t == 1:
                    act.wait_ge(pw_lo_ok, 1)
                copy(gain[:, :] if t % 2 else scr[:, 0, :], pair(2 * (t % 2)), e_ok,
                     scale=rs[:, 4 * TT + t:4 * TT + t + 1])

            e_square(0)
            for t in range(1, TT):
                e_square(t)
                e_scale(t - 1)
            e_scale(TT - 1)
            act.wait_ge(e_mm, TT)
            for r in range(2):
                split_row(r, ws_hi[:, r, :], 5 * DMA)
            act.wait_ge(const_ok, 2)
            for g in range(GROUPS):
                act.wait_ge(q_mm, g + 1)
                act.wait_ge(q_lo_ok, g) if g else act.wait_ge(p_lo_ok, KP)
                act.activation(scr[:, 2, :], pair(2 * (g % 2)), ACT.Copy, scale=pscale[:, g:g + 1])\
                    .then_inc(q_copied, 1)
                copy(act_hi[:, KC + g, :], pair(2 * (g % 2)), q_copied, scale=pscale[:, g:g + 1])
            for k in range(4):
                split_row((2, 3, 0, 1)[k], bs_hi[:, k, :], (5 if k < 2 else 6) * DMA)

            def mix_rows(h):
                for c in range(KC):
                    n = KC * h + c
                    b = n % 4
                    y, s = scr[:, 0, (n % 2) * BANK:(n % 2 + 1) * BANK], scr[:, 1, (n % 2) * BANK:(n % 2 + 1) * BANK]
                    act.wait_ge(lnb_mm, n + 1)
                    if n >= 2:
                        act.wait_ge(mix_lo_ok, n - 1)
                    act.activation(y, ps[:, 4 + b, :], ACT.Identity, bias=lnb[:, c:c + 1], scale=lng[:, c:c + 1])
                    act.activation(s, ps[:, 4 + b, :], ACT.Sigmoid, bias=lnb[:, c:c + 1],
                                   scale=lng[:, c:c + 1]).then_inc(y_ok, 1)
                    act.wait_ge(silu_ok, n + 1)
                    copy(act_hi[:, c, h * BANK:(h + 1) * BANK], y, mix_hi_ok)

            act.wait_ge(e_stored[0], DMA * (TT // 2))
            mix_rows(0)

            def square_after(t, norm, ready, count):
                act.wait_ge(ready, count)
                act.wait_ge(ss_ok, norm * TT + t)
                square(t, norm)

            square_after(0, 1, rows_added, 2)
            square_after(1, 1, rows_added, 4)
            mix_rows(1)
            turned_hi(0, 1)
            for t in range(2, TT):
                turned_hi(t - 1, 1)
                square_after(t, 1, rows_added, 2 * (t + 1))
            act.wait_ge(rows_done, 2 * TT)
            for m in range(4):
                split_cols(m, 6 * DMA + (DMA if m % 2 == 0 else 0))
            turned_hi(TT - 1, 1)

            def ffn(i, last):
                for f in range(2):
                    act.wait_ge(rawb_in, i * DMA + 2 * DMA)
                    act.wait_ge(rows_done, i * 16 + 16)
                    copy(bs_hi[:, f, :], raw_b[:, f, :], wd_hi)
                for f in range(2):
                    for h in range(HALVES):
                        s = 2 * f + h
                        act.wait_ge(gu_mm, i * 4 + (s + 1))
                        act.activation(wide[:, 0, (s % 2) * BANK:(s % 2 + 1) * BANK], ps[:, 2 * (s % 2), :],
                                       ACT.Sigmoid).then_inc(sig_ok, 1)
                        act.wait_ge(in_ok, i * 4 + (s + 1))
                        copy(bs_hi[:, 2 + f, h * BANK:(h + 1) * BANK],
                             wide[:, 1, (s % 2) * BANK:(s % 2 + 1) * BANK], in_hi)
                    act.wait_ge(gu_mm, i * 4 + (2 * f + 2))
                    for m in (2 * f, 2 * f + 1):
                        if last:
                            split_row(m, ws_hi[:, m, :], ((8 if m < 2 else 7) + NCH - 1) * DMA)
                        else:
                            split_cols(m, i * DMA + (8 if m % 2 == 0 else 7) * DMA)

            with act.Fori(0, NCH - 1) as i:
                ffn(i, False)
            ffn(NCH - 1, True)
            square_after(0, 2, rows_added, 16 * NCH + 2)
            for t in range(1, TT):
                square_after(t, 2, rows_added, 16 * NCH + 2 * (t + 1))
                turned_hi(t - 1, 2)
            act.wait_ge(rows_done, 16 * (NCH + 1))
            for k in range(4):
                act.wait_ge(raw_in[k // 2], (8 if k < 2 else 7) * DMA + NCH * DMA)
                copy(bs_hi[:, k, :], raw[:, k, :], pg_hi)

            def gate(t):
                act.wait_ge(pg_mm, t + 1)
                if t >= 2:
                    act.wait_ge(res_ok, t - 1)
                act.activation(wide[:, t % 2, 0:D], pair(2 + 2 * (t % 3)), ACT.Sigmoid).then_inc(gate_ok, 1)

            gate(0)
            turned_hi(TT - 1, 2)
            for t in range(TT):
                if t:
                    gate(t)
                square_after(t, 3, res_ok, t + 1)

        @block.tensor
        def _(pe):
            def product(dst, w_hi_, w_lo_, m_hi, m_lo, start, stop):
                pe.matmul(dst, w_lo_, m_hi, start=start, stop=False)
                pe.matmul(dst, w_hi_, m_lo, start=False, stop=False)
                return pe.matmul(dst, w_hi_, m_hi, start=False, stop=stop)

            def cols_mm(bank, m, h, kk=range(KD)):
                for k in kk:
                    w = slice(k * P, (k + 1) * P)
                    mv_ = slice(h * BANK, (h + 1) * BANK)
                    last = product(ps[:, bank, :], ws_hi[:, m, w], ws_lo[:, m, w],
                                   act_hi[:, k, mv_], act_lo[:, k, mv_], k == 0, k == KD - 1)
                return last

            def rows_mm(bank0, t, ks, stripes, first, final):
                lasts = []
                for d in range(2):
                    for j, k in enumerate(ks):
                        hi_, lo_, r = stripes(k)
                        c = slice(d * BANK, (d + 1) * BANK)
                        last = product(ps[:, bank0 + d, :], act_hi[:, k, t * P:(t + 1) * P],
                                       act_lo[:, k, t * P:(t + 1) * P], hi_[:, r, c], lo_[:, r, c],
                                       first and j == 0, final and j == len(ks) - 1)
                    lasts.append(last)
                return lasts

            def turn(t, norm, waits=()):
                n = norm * TT + t
                pe.wait_ge(xn_ok, n + 1)
                for j in range(2):
                    if n:
                        pe.wait_ge(act_lo_ok, 2 * n + j - 1)
                    for q in range(4):
                        k = 4 * j + q
                        ins = pe.transpose(ps[:, TURN_BANK[norm] + j, q * P:(q + 1) * P],
                                           scr[:, n % 2, k * P:(k + 1) * P], ident[:, :])
                    ins.then_inc(turned, 1)

            pe.wait_ge(ident_ok, 2)
            for t in range(TT):
                turn(t, 0)

            def up_mm(m0, waits, done):
                for h in range(HALVES):
                    waits(h)
                    cols_mm(2 * h, m0, h)
                    cols_mm(2 * h + 1, m0 + 1, h).then_inc(done, 1)

            pe.wait_ge(const_in, 5 * DMA)
            for c in range(KC):
                pe.transpose(ps[:, 4, c * 32:c * 32 + TAPS], scr[0:TAPS, 2, c * P:(c + 1) * P],
                             ident[0:TAPS, 0:TAPS])
            pe.transpose(ps[:, 5, 0:4 * KC], scr[0:4 * KC, 2, C:C + P], ident[0:4 * KC, 0:4 * KC])\
              .then_inc(const_mm, 1)
            for c in range(KC):
                pe.wait_ge(w_lo, 2 * c + 2)

                def waits(h, c=c):
                    if c == 0:
                        pe.wait_ge(act_lo_ok, 2 * HT * (h + 1))
                    else:
                        pe.wait_ge(ab_ev, HALVES * c + h - 1)

                up_mm(2 * (c % 2), waits, ab_mm)

            pe.wait_ge(ab_ev, HALVES * KC)
            for s_, g in enumerate((0, 2, 1, 3)):
                pe.wait_ge(w_lo, 8 + s_ + 1)
                if s_ >= 2:
                    pe.wait_ge(v_ev, s_ - 1)
                for h in range(HALVES):
                    last = cols_mm(2 * (s_ % 2) + h, s_, h)
                last.then_inc(v_mm, 1)

            pe.wait_ge(rawb_in, DMA)
            pe.wait_ge(v_ev, 4)
            pt = raw_b[:, :, :].rearrange("p a (t d) -> p (a t) d", d=DP)
            for k in range(KP):
                for h in range(HALVES):
                    for q in range(HT):
                        ins = pe.transpose(ps[:, 2 * k + h, q * P:(q + 1) * P],
                                           pt[:, h * HT + q, k * P:(k + 1) * P], ident[:, :])
                    ins.then_inc(p_turned, 1)

            pe.wait_ge(p_lo_ok, KP)
            pe.wait_ge(w_lo, N_IN + N_PLE)
            for t in range(TT):
                if t >= 2:
                    pe.wait_ge(e_ok, t - 1)
                rows_mm(2 * (t % 2), t, range(KP), lambda k: (ws_hi, ws_lo, k), True, True)[-1]\
                    .then_inc(e_mm, 1)

            pe.wait_ge(pw_lo_ok, 1)
            pe.wait_ge(pooled_lo, GROUPS)
            for g in range(GROUPS):
                pe.wait_ge(e_ok, TT - 1 + g) if g < 2 else pe.wait_ge(q_copied, 2 * (g - 1))
                w = slice(g * P, (g + 1) * P)
                for h in range(HALVES):
                    mv_ = slice(h * BANK, (h + 1) * BANK)
                    last = product(ps[:, 2 * (g % 2) + h, :], act_hi[:, 2, w], act_lo[:, 2, w],
                                   bs_hi[:, g, mv_], bs_lo[:, g, mv_], True, True)
                last.then_inc(q_mm, 1)

            def wo_stripe(k):
                return (ws_hi, ws_lo, k - 4) if k >= 4 else (bs_hi, bs_lo, k)

            def rows_out(bank0, t, ks, stripes, first, final):
                for ins in rows_mm(bank0, t, ks, stripes, first, final):
                    if final:
                        ins.then_inc(rows_done, 1)

            pe.wait_ge(q_lo_ok, GROUPS)
            pe.wait_ge(w_lo, N_IN + N_PLE + 4)
            for t in range(2):
                rows_out(2 * t, t, range(4, 8), wo_stripe, True, False)

            def conv_turn(t):
                if t >= 4:
                    pe.wait_ge(y_ok, t - 3)
                for c in range(KC):
                    ins = pe.transpose(ps[:, 4 + t % 4, c * P:(c + 1) * P],
                                       conv_o[:, c, t * P:(t + 1) * P], ident[:, :])
                ins.then_inc(lnf_mm, 1)

            def normed_turn(h):
                pe.wait_ge(n_ok, HT * (h + 1))
                for c in range(KC):
                    for q in range(HT):
                        at = (h * HT + q) * C + c * P
                        ins = pe.transpose(ps[:, 4 + c, q * P:(q + 1) * P], wide_f[:, at:at + P], ident[:, :])
                    ins.then_inc(lnb_mm, 1)

            pe.wait_ge(taps_done, (TAPS + 1) * KC)
            for t in range(HT):
                conv_turn(t)
            normed_turn(0)
            for t in range(HT, TT):
                conv_turn(t)
            pe.wait_ge(mix_lo_ok, KC)
            pe.wait_ge(w_lo, GU0)
            for t in range(2):
                rows_out(2 * t, t, range(4), wo_stripe, False, True)
            normed_turn(1)
            pe.wait_ge(y_ok, 2 * KC)
            turn(0, 1)
            for t in range(2, TT):
                if t == HT:
                    pe.wait_ge(mix_lo_ok, 2 * KC)
                if t >= 3:
                    pe.wait_ge(rows_added, 2 * (t - 2))
                rows_out(2 * (t % 3), t, (4, 5, 6, 7, 0, 1, 2, 3), wo_stripe, True, True)
                turn(t - 1, 1)
            turn(TT - 1, 1)
            pe.wait_ge(rows_added, 2 * TT)

            def down(i, t, bank_of):
                h = t // HT
                if t % HT == 0:
                    pe.wait_ge(in_lo, i * 4 + (3 + h))
                for d in range(2):
                    n = 2 * t + d
                    pe.wait_ge(rows_added, i * 16 + (16 + n - 3))
                    for f in range(2):
                        last = product(ps[:, 4 + n % 4, :], bs_hi[:, 2 + f, t * P:(t + 1) * P],
                                       bs_lo[:, 2 + f, t * P:(t + 1) * P],
                                       bs_hi[:, f, d * BANK:(d + 1) * BANK], bs_lo[:, f, d * BANK:(d + 1) * BANK],
                                       f == 0, f == 1)
                    last.then_inc(rows_done, 1)

            def gate_up(i, first):
                for f in range(2):
                    pe.wait_ge(w_lo, i * 4 + (GU0 + 2 * f + 2))

                    def waits(h):
                        if f:
                            pe.wait_ge(in_ok, i * 4 + (h + 1))
                        elif first:
                            pe.wait_ge(act_lo_ok, 2 * (TT + HT * (h + 1)))

                    up_mm(2 * f, waits, gu_mm)

            def chunk(i):
                gate_up(i, True)
                pe.wait_ge(wd_lo, i * 2 + 2)
                for t in range(TT):
                    down(i, t, None)

            with pe.Fori(0, NCH - 1) as i:
                chunk(i)
            gate_up(NCH - 1, False)
            pe.wait_ge(wd_lo, 2 * NCH)
            for t in range(TT):
                down(NCH - 1, t, None)
                if t:
                    turn(t - 1, 2)

            def pg_stripe(k):
                return (ws_hi, ws_lo, k) if k < 4 else (bs_hi, bs_lo, k - 4)

            for t in range(TT):
                b = 2 + 2 * (t % 3)
                pe.wait_ge(act_lo_ok, 2 * (2 * TT + t + 1))
                if t == 0:
                    pe.wait_ge(w_lo, GU0 + 4 * NCH + 4)
                    rows_mm(b, t, range(4), pg_stripe, True, False)
                    turn(TT - 1, 2)
                    pe.wait_ge(pg_lo, 4)
                    rows_mm(b, t, range(4, 8), pg_stripe, False, True)[-1].then_inc(pg_mm, 1)
                    continue
                if t in (1, 2):
                    pe.wait_ge(rows_added, 16 * (NCH + 1))
                elif t >= 3:
                    pe.wait_ge(gate_ok, t - 2)
                rows_mm(b, t, range(8), pg_stripe, True, True)[-1].then_inc(pg_mm, 1)

        @block.vector
        def _(dve):
            def lo(dst, src, hi, done):
                dve.tensor_tensor(dst, src, hi.bitcast(F32), ALU.subtract).then_inc(done, 1)

            def turned_lo(t, norm):
                n = norm * TT + t
                for j in range(2):
                    dve.wait_ge(act_hi_ok, 2 * n + j + 1)
                    at = (slice(None), slice(4 * j, 4 * j + 4), slice(t * P, (t + 1) * P))
                    lo(act_lo[at], ps[:, TURN_BANK[norm] + j, :].rearrange("p (k s) -> p k s", k=4),
                       act_hi[at], act_lo_ok)

            def normed(t, norm, gains):
                n = norm * TT + t
                if t == 0:
                    dve.wait_ge(gain_in, gains * DMA)
                dve.wait_ge(rs_ok, n + 1)
                if n >= 2:
                    dve.wait_ge(turned, 2 * n - 2)
                dve.scalar_tensor_tensor(out=scr[:, n % 2, :], in0=xres[:, t, :], scalar=rs[:, n:n + 1],
                                         in1=gain[:, :], op0=ALU.mult, op1=ALU.mult).then_inc(xn_ok, 1)

            for t in range(TT):
                normed(t, 0, 1)
                if t:
                    turned_lo(t - 1, 0)
            turned_lo(TT - 1, 0)
            dve.wait_ge(const_mm, 1)
            dve.tensor_copy(convw[:, :].rearrange("p (c k) -> p c k", c=KC)[:, :, 0:TAPS],
                            ps[:, 4, 0:KC * 32].rearrange("p (c k) -> p c k", c=KC)[:, :, 0:TAPS])\
                .then_inc(const_ok, 1)
            dve.tensor_copy(cvec[:, :], ps[:, 5, 0:4 * KC]).then_inc(const_ok, 1)
            dve.wait_ge(const_ok, 2)

            even, odd = pair(4), pair(6)
            last_odd = TAPS - 1 if TAPS % 2 == 0 else TAPS - 2
            with dve.Fori(0, KC) as c:
                dve.wait_ge(u_ok, c * HALVES + HALVES)
                conv_c = resid[:, bass.ds(c * SEQ + KC * UW, SEQ)]
                for k in range(TAPS):
                    acc = odd if k % 2 else even
                    u = resid[:, bass.ds(c * UW + k, SEQ)]
                    w = convw[:, bass.ds(c * 32 + k, 1)]
                    if k < 2:
                        ins = dve.tensor_scalar(acc, u, w, None, ALU.mult)
                    else:
                        dve.wait_ge(taps_done, c * (TAPS + 1) + (k - 1))
                        ins = dve.scalar_tensor_tensor(out=conv_c if k == last_odd else acc, in0=u,
                                                       scalar=w, in1=acc,
                                                       op0=ALU.mult, op1=ALU.add)
                    ins.then_inc(taps_done, 1)
                dve.wait_ge(taps_done, c * (TAPS + 1) + TAPS)
                dve.scalar_tensor_tensor(out=conv_c, in0=even, scalar=cvec[:, bass.ds(c, 1)], in1=conv_c,
                                         op0=ALU.add, op1=ALU.add).then_inc(taps_done, 1)
                dve.wait_ge(taps_done, c * (TAPS + 1) + (TAPS + 1))

            def stats(t):
                b = 4 + t % 4
                dve.wait_ge(lnf_mm, t + 1)
                dve.bn_stats(bst[:, t, :], ps[:, b, :]).then_inc(bn_ok, 1)
                dve.wait_ge(bn_ok, t + 1)
                dve.bn_aggr(mv[:, t, :], bst[:, t, :]).then_inc(mv_ok, 1)
                dve.wait_ge(mv_ok, t + 1)
                dve.tensor_scalar(mv[:, t, 1:2], mv[:, t, 1:2], EPS, None, ALU.add).then_inc(var_ok, 1)

            def center(t):
                dve.wait_ge(lrs_ok, t + 1)
                dve.tensor_scalar(wide_f[:, t * C:(t + 1) * C], ps[:, 4 + t % 4, :], mv[:, t, 0:1],
                                  lrs[:, t:t + 1], ALU.subtract, ALU.mult).then_inc(n_ok, 1)

            def ln_tiles(first):
                for t in range(first, first + HT):
                    stats(t)
                    if t > first:
                        center(t - 1)
                center(first + HT - 1)

            def silu(h):
                for c in range(KC):
                    n = KC * h + c
                    a = slice((n % 2) * BANK, (n % 2 + 1) * BANK)
                    dve.wait_ge(y_ok, n + 1)
                    dve.tensor_tensor(scr[:, 0, a], scr[:, 0, a], scr[:, 1, a], ALU.mult).then_inc(silu_ok, 1)
                    dve.wait_ge(mix_hi_ok, n + 1)
                    at = (slice(None), c, slice(h * BANK, (h + 1) * BANK))
                    lo(act_lo[at], scr[:, 0, a], act_hi[at], mix_lo_ok)

            def add_x(t):
                dve.wait_ge(x_in[t], 2 * DMA)
                for d in range(2):
                    dve.wait_ge(rows_done, 2 * t + d + 1)
                    c = slice(d * BANK, (d + 1) * BANK)
                    dve.tensor_tensor(xres[:, t, c], ps[:, 2 * (t % 3) + d, :], raw_b[:, t % 2, c], ALU.add)\
                       .then_inc(rows_added, 1)

            ln_tiles(0)
            silu(0)
            ln_tiles(HT)
            add_x(0)
            add_x(1)
            silu(1)
            dve.wait_ge(mix_lo_ok, 2 * KC)
            normed(0, 1, 3)
            turned_lo(0, 1)
            normed(1, 1, 3)
            for t in range(2, TT):
                add_x(t)
                turned_lo(t - 1, 1)
                normed(t, 1, 3)
            turned_lo(TT - 1, 1)

            def inner(i):
                for s in range(4):
                    f, h = divmod(s, 2)
                    a = slice((s % 2) * BANK, (s % 2 + 1) * BANK)
                    b = 2 * (s % 2)
                    dve.wait_ge(sig_ok, i * 4 + (s + 1))
                    dve.tensor_tensor(wide[:, 0, a], ps[:, b, :], wide[:, 0, a], ALU.mult).then_inc(gs_ok, 1)
                    dve.wait_ge(gs_ok, i * 4 + (s + 1))
                    if s >= 2:
                        dve.wait_ge(in_lo, i * 4 + (s - 1))
                    dve.tensor_tensor(wide[:, 1, a], wide[:, 0, a], ps[:, b + 1, :], ALU.mult).then_inc(in_ok, 1)
                    dve.wait_ge(in_hi, i * 4 + (s + 1))
                    at = (slice(None), 2 + f, slice(h * BANK, (h + 1) * BANK))
                    lo(bs_lo[at], wide[:, 1, a], bs_hi[at], in_lo)
                dve.wait_ge(in_lo, i * 4 + 4)

            def add_rows(i, t):
                for d in range(2):
                    n = 2 * t + d
                    dve.wait_ge(rows_done, i * 16 + (16 + n + 1))
                    x_ = xres[:, t, d * BANK:(d + 1) * BANK]
                    dve.tensor_tensor(x_, x_, ps[:, 4 + n % 4, :], ALU.add).then_inc(rows_added, 1)

            with dve.Fori(0, NCH - 1) as i:
                inner(i)
                for t in range(TT):
                    add_rows(i, t)
            inner(NCH - 1)
            add_rows(NCH - 1, 0)
            normed(0, 2, 4)
            for t in range(1, TT):
                add_rows(NCH - 1, t)
                turned_lo(t - 1, 2)
                normed(t, 2, 4)
            for k in range(4):
                dve.wait_ge(pg_hi, k + 1)
                lo(bs_lo[:, k, :], raw[:, k, :], bs_hi[:, k, :], pg_lo)
            turned_lo(TT - 1, 2)

            def gated(t):
                g = wide[:, t % 2, 0:D]
                dve.wait_ge(gate_ok, t + 1)
                dve.wait_ge(eg_ok, t + 1)
                dve.tensor_tensor(g, g, wide[:, 2 + t % 2, 0:D], ALU.mult).then_inc(ge_ok, 1)
                dve.wait_ge(ge_ok, t + 1)
                dve.tensor_tensor(xres[:, t, :], xres[:, t, :], g, ALU.add).then_inc(res_ok, 1)

            def final(t):
                dve.wait_ge(rs_ok, 3 * TT + t + 1)
                if t >= 2:
                    dve.wait_ge(out_stored[t % 2], DMA * (t // 2))
                dve.scalar_tensor_tensor(out=scr[:, t % 2, :], in0=xres[:, t, :],
                                         scalar=rs[:, 3 * TT + t:3 * TT + t + 1], in1=raw_b[:, 1, :],
                                         op0=ALU.mult, op1=ALU.mult).then_inc(fin_ok, 1)

            dve.wait_ge(gfin_in, 2 * DMA)
            dve.wait_ge(turned, 2 * 3 * TT)
            for t in range(TT):
                gated(t)
                if t:
                    final(t - 1)
            final(TT - 1)


INPUTS = ["x", "p", "g_mix", "w_in", "conv_w", "conv_b", "ln_g", "ln_b", "pool_w", "pool_scale", "w_out",
          "g_ffn", "w_gate_up", "w_down", "g_ple_gate", "w_ple_gate", "w_ple_up", "g_ple_post", "g_final"]


def kernel(**inputs):
    import concourse.bacc as bacc
    from concourse.bass_utils import run_bass_kernel_spmd

    nc = bacc.Bacc("TRN2", target_bir_lowering=False, num_devices=1, dynamic_dma_scratch_size=1024)
    arrays, args = {}, {}
    for name in INPUTS:
        a = np.ascontiguousarray(inputs[name])
        arrays[f"in_{name}"] = a
        args[name] = nc.dram_tensor(f"in_{name}", a.shape, mybir.dt.from_np(a.dtype), kind="ExternalInput").ap()
    out = nc.dram_tensor("out_x", inputs["x"].shape, F32, kind="ExternalOutput").ap()
    hybrid_block(nc, out=out, **args)
    return run_bass_kernel_spmd(nc, [arrays], core_ids=[0]).results[0]["out_x"]
```

```python
from contextlib import ExitStack

import numpy as np

import concourse.bass as bass
from concourse import mybir

F32, F32R, BF16 = mybir.dt.float32, mybir.dt.float32r, mybir.dt.bfloat16
ALU, ACT = mybir.AluOpType, mybir.ActivationFunctionType

P = 128
EPS = 1e-6
BANK = 512
HEADPAD = 16
DMA = 16


def hybrid_block(nc, x, p, g_mix, w_in, conv_w, conv_b, ln_g, ln_b, pool_w, pool_scale, w_out,
                 g_ffn, w_gate_up, w_down, g_ple_gate, w_ple_gate, w_ple_up, g_ple_post,
                 g_final, out):
    SEQ, D = x.shape[1], x.shape[2]
    C = conv_w.shape[2]
    TAPS = conv_w.shape[1]
    GROUPS = pool_w.shape[1]
    F = w_down.shape[1]
    DP = p.shape[3]
    TT = SEQ // P
    KD = D // P
    KC = C // P
    KP = DP // P
    HALVES = SEQ // BANK
    HT = TT // HALVES
    NCH = F // (2 * P)
    PAD = TAPS - 1
    UW = PAD + SEQ
    assert (SEQ, D, C, KD, KC, KP, GROUPS, HALVES) == (1024, 1024, 512, 8, 4, 2, 4, 2)
    assert F == NCH * 2 * P

    x_v = x[0].rearrange("(t p) d -> t p d", p=P)
    out_v = out[0].rearrange("(t p) d -> t p d", p=P)
    p_v = p[0, 0].rearrange("(t p) d -> p t d", p=P)
    w_in_v = w_in[0].rearrange("(k p) n -> p k n", p=P)
    w_gu_v = w_gate_up[0].rearrange("(k p) n -> p k n", p=P)
    w_out_v = w_out[0].rearrange("(k p) n -> p k n", p=P)
    w_dn_v = w_down[0].rearrange("(f p) n -> p f n", p=P)
    w_pg_v = w_ple_gate[0].rearrange("(k p) n -> p k n", p=P)
    w_pu_v = w_ple_up[0].rearrange("(k p) n -> p k n", p=P)
    e_dram = nc.dram_tensor("e_scratch", (TT, P, D), F32, kind="Internal").ap()

    with ExitStack() as ctx:
        def sb(name, shape, dt=F32):
            return ctx.enter_context(nc.sbuf_tensor(name, shape, dt))

        def sem(name):
            return ctx.enter_context(nc.semaphore(name))

        resid = sb("resid", [P, KC * UW + KC * SEQ])
        xres = resid[:, 0:TT * D].rearrange("p (t d) -> p t d", t=TT)
        u_all = resid[:, 0:KC * UW].rearrange("p (c s) -> p c s", c=KC)
        conv_o = resid[:, KC * UW:KC * UW + KC * SEQ].rearrange("p (c s) -> p c s", c=KC)
        act_hi = sb("act_hi", [P, KD, SEQ], F32R)
        act_lo = sb("act_lo", [P, KD, SEQ], F32R)
        ws_hi = sb("ws_hi", [P, 4, 1024], F32R)
        ws_lo = sb("ws_lo", [P, 4, 1024], F32R)
        bs_hi = sb("bs_hi", [P, 4, 1024], F32R)
        bs_lo = sb("bs_lo", [P, 4, 1024], F32R)
        raw = sb("raw", [P, 4, 1024])
        raw_b = sb("raw_b", [P, 2, 1024])
        wide = sb("wide", [P, 4, SEQ + HEADPAD])
        wide_f = wide[:, :, :].rearrange("p a b -> p (a b)")
        scr = sb("scr", [P, 3, 1024])
        gain = sb("gain", [P, D])
        junk = sb("junk", [P, 1024], BF16)
        ident = sb("ident", [P, P])
        convw = sb("convw", [P, KC * 32])
        cvec = sb("cvec", [P, 4 * KC])
        qscale = sb("qscale", [P, GROUPS])
        convb, lng, lnb, pscale = (cvec[:, KC * n:KC * (n + 1)] for n in range(4))
        head = sb("head", [P, GROUPS, HEADPAD])
        pw_raw = sb("pw_raw", [P, GROUPS * P])
        neg_half = sb("neg_half", [P, 1])
        ss = sb("ss", [P, 5 * TT])
        rs = sb("rs", [P, 5 * TT])
        bst = sb("bst", [P, TT, 6])
        mv = sb("mv", [P, TT, 2])
        lrs = sb("lrs", [P, TT])
        ps = ctx.enter_context(nc.psum_tensor("ps", [P, 8, BANK], F32))

        def cols_of(w, m):
            piece = w[:, 2 * (m % 2):2 * (m % 2) + 2, :].rearrange("p a (b n) -> p (a b) n", n=2 * P)
            return piece[:, :, (m // 2) * P:(m // 2 + 1) * P]

        def pair(b):
            return ps[:, b:b + 2, :].rearrange("p a b -> p (a b)")

        x_in = [sem(f"x_in{t}") for t in range(TT)]
        const_in = sem("const_in")
        gain_in = sem("gain_in")
        pw_in = sem("pw_in")
        first_in = [sem(f"first_in{j}") for j in range(2)]
        raw_in = [sem(f"raw_in{j}") for j in range(2)]
        rawb_in = sem("rawb_in")
        e_stored = [sem(f"e_stored{j}") for j in range(2)]
        e_in = [sem(f"e_in{j}") for j in range(2)]
        gfin_in = sem("gfin_in")
        out_stored = [sem(f"out_stored{j}") for j in range(2)]
        ident_ok = sem("ident_ok")
        tables_ok = sem("tables_ok")
        upad_ok = sem("upad_ok")
        ss_ok = sem("ss_ok")
        ms_ok = sem("ms_ok")
        rs_ok = sem("rs_ok")
        xn_ok = sem("xn_ok")
        turned = sem("turned")
        act_hi_ok = sem("act_hi_ok")
        act_lo_ok = sem("act_lo_ok")
        w_hi = sem("w_hi")
        w_lo = sem("w_lo")
        wd_hi = sem("wd_hi")
        wd_lo = sem("wd_lo")
        ab_mm = sem("ab_mm")
        ab_ev = sem("ab_ev")
        u_ok = sem("u_ok")
        taps_in = sem("taps_in")
        taps_sum = sem("taps_sum")
        taps_done = sem("taps_done")
        v_mm = sem("v_mm")
        v_ev = sem("v_ev")
        e_sq = sem("e_sq")
        e_ms = sem("e_ms")
        e_rs = sem("e_rs")
        wv_ok = sem("wv_ok")
        mix_hi_ok = sem("mix_hi_ok")
        win_step = sem("win_step")
        head_ok = sem("head_ok")
        pooled_ok = sem("pooled_ok")
        pooled_hi = sem("pooled_hi")
        pooled_lo = sem("pooled_lo")
        pw_hi_ok = sem("pw_hi_ok")
        pw_lo_ok = sem("pw_lo_ok")
        p_turned = sem("p_turned")
        p_copied = sem("p_copied")
        p_lo_ok = sem("p_lo_ok")
        e_mm = sem("e_mm")
        e_ok = sem("e_ok")
        q_mm = sem("q_mm")
        q_copied = sem("q_copied")
        q_lo_ok = sem("q_lo_ok")
        lnf_mm = sem("lnf_mm")
        bn_ok = sem("bn_ok")
        mv_ok = sem("mv_ok")
        var_ok = sem("var_ok")
        lrs_ok = sem("lrs_ok")
        n_ok = sem("n_ok")
        lnb_mm = sem("lnb_mm")
        y_ok = sem("y_ok")
        silu_ok = sem("silu_ok")
        mix_lo_ok = sem("mix_lo_ok")
        const_mm = sem("const_mm")
        const_ok = sem("const_ok")
        rows_done = sem("rows_done")
        rows_added = sem("rows_added")
        gu_mm = sem("gu_mm")
        sig_ok = sem("sig_ok")
        gs_ok = sem("gs_ok")
        in_ok = sem("in_ok")
        in_hi = sem("in_hi")
        in_lo = sem("in_lo")
        pg_hi = sem("pg_hi")
        pg_lo = sem("pg_lo")
        pg_mm = sem("pg_mm")
        gate_ok = sem("gate_ok")
        eg_ok = sem("eg_ok")
        ge_ok = sem("ge_ok")
        res_ok = sem("res_ok")
        fin_ok = sem("fin_ok")

        N_IN, N_PLE, N_WO = 12, KP, KD
        N_TABLES = 2 + sum(2 << g for g in range(GROUPS))
        GU0 = N_IN + N_PLE + N_WO
        S_B, S_PLE, S_V, S_WOQ, S_WOU = 4, 8, 10, 14, 18
        V_STRIPE, V_GROUP = (2, 0, 3, 1), (3, 2, 1, 0)
        AB = [(0, c) for c in range(KC)] + [(1, c) for c in (2, 3, 0, 1)]
        LN_BANK = (6, 7, 4, 5)
        PG_BANK = (4, 6, 2)
        Q_AFTER = (3, 6)
        WO_BANK = (0, 2, 6, 0, 2, 0, 2, 0)

        OWN = 4
        OPS = TAPS - OWN + 1

        def turn_bank(norm, t):
            return (6 - 2 * (t % 2), 6, 2 * (t % 2))[norm]

        def ab_at(c):
            return (ws_hi, ws_lo, 2 * c) if c < 2 else (bs_hi, bs_lo, 2 * (c - 2))

        def q_place(s):
            return (wide[:, 0, 0:SEQ], wide[:, 0, 0:SEQ], wide[:, 3, 0:SEQ], scr[:, 0, :])[s]

        def sigmoid_b(n):
            return wide[:, 3, HEADPAD + (n % 2) * BANK:HEADPAD + (n % 2 + 1) * BANK]

        def silu_place(n):
            h, c = divmod(n, KC)
            if h:
                return wide[:, c, 0:BANK], wide[:, c, BANK:2 * BANK]
            return conv_o[:, c, 0:BANK], u_all[:, c, 0:BANK]

        def cols_stripe(w, m):
            return w[:, m, :].rearrange("p (k n) -> p k n", k=KD)

        block = ctx.enter_context(nc.Block())

        @block.sync
        def _(sp):
            def load_gain(g):
                sp.dma_start(gain[:, :], g.partition_broadcast(P)).then_inc(gain_in, DMA)

            def load_cols(view, lo, hi):
                for j, first in enumerate((lo, hi)):
                    sp.dma_start(raw[:, 2 * j:2 * j + 2, :].rearrange("p a (b n) -> p (a b) n", n=256),
                                 view[:, :, bass.ds(first, 256)]).then_inc(raw_in[j], DMA)

            def load_pair(half, signals):
                for j, first in enumerate((0, C)):
                    piece = raw[:, 2 * j:2 * j + 2, :].rearrange("p a (b n) -> p (a b) n", n=256)
                    sp.dma_start(piece[:, :, half * P:(half + 1) * P],
                                 w_in_v[:, :, first + half * P:first + (half + 1) * P]).then_inc(signals[j], DMA)

            def load_rows(j, rows):
                sp.dma_start(raw[:, 2 * j:2 * j + 2, :], rows).then_inc(raw_in[j], DMA)

            def load_x(t, dst):
                sp.dma_start(dst, x_v[t]).then_inc(x_in[t], DMA)

            load_x(0, xres[:, 0, :])
            load_gain(g_mix[0])
            for t in range(1, 4):
                load_x(t, xres[:, t, :])
            load_pair(0, first_in)
            load_x(4, xres[:, 4, :])
            load_x(5, xres[:, 5, :])
            load_pair(1, raw_in)
            sp.dma_start(scr[0:TAPS, 2, 0:C], conv_w[0]).then_inc(const_in, DMA)
            for n, src in enumerate((conv_b, ln_g, ln_b, pool_scale)):
                sp.dma_start(scr[KC * n:KC * (n + 1), 2, C:C + P], src[0].rearrange("(c p) -> c p", p=P))\
                  .then_inc(const_in, DMA)
            load_x(6, xres[:, 6, :])
            load_x(7, xres[:, 7, :])
            sp.wait_ge(w_lo, S_B)
            load_cols(w_in_v, 256, C + 256)
            sp.dma_start(raw_b[:, :, :].rearrange("p a (t d) -> p (a t) d", d=DP), p_v).then_inc(rawb_in, DMA)
            sp.dma_start(pw_raw[:, :].rearrange("p (g d) -> p g d", g=GROUPS),
                         pool_w[0].rearrange("g c d -> c g d")).then_inc(pw_in, DMA)
            sp.wait_ge(w_lo, S_PLE)
            load_cols(w_in_v, 2 * C + 256, 2 * C)
            sp.wait_ge(p_turned, KP)
            sp.dma_start(raw_b[:, :, :], w_pu_v).then_inc(rawb_in, DMA)
            sp.wait_ge(w_lo, S_WOQ)
            load_rows(0, w_out_v[:, 4:6, :])
            load_rows(1, w_out_v[:, 6:8, :])
            for t in range(TT):
                sp.wait_ge(e_ok, t + 1)
                sp.dma_start(e_dram[t], raw_b[:, t % 2, :]).then_inc(e_stored[t % 2], DMA)
            sp.wait_ge(w_lo, S_WOQ + 2)
            load_rows(1, w_out_v[:, 2:4, :])
            sp.wait_ge(w_lo, S_WOQ + 4)
            load_rows(0, w_out_v[:, 0:2, :])
            for t in range(2):
                sp.wait_ge(e_stored[t], DMA * (TT // 2))
                load_x(t, raw_b[:, t, :])
            sp.wait_ge(taps_done, (2 * KC - 1) * OPS + 2)
            load_gain(g_ffn[0])
            sp.wait_ge(w_lo, GU0)
            load_cols(w_gu_v, 0, F)
            for t in range(2, TT):
                sp.wait_ge(rows_added, 2 * (t - 1))
                load_x(t, raw_b[:, t % 2, :])
            sp.wait_ge(rows_added, 2 * TT)
            sp.dma_start(raw_b[:, :, :], w_dn_v[:, 0:2, :]).then_inc(rawb_in, DMA)
            sp.wait_ge(xn_ok, 2 * TT)
            load_gain(g_ple_gate[0])
            with sp.Fori(0, NCH - 1) as i:
                sp.wait_ge(w_lo, i * 4 + (GU0 + 4))
                load_cols(w_gu_v, (i + 1) * 256, (i + 1) * 256 + F)
                sp.wait_ge(wd_lo, i * 2 + 2)
                sp.dma_start(raw_b[:, :, :], w_down[0][bass.ds((i + 1) * 256, 256), :]
                             .rearrange("(f p) n -> p f n", p=P)).then_inc(rawb_in, DMA)
            sp.wait_ge(w_lo, GU0 + 4 * NCH)
            load_rows(0, w_pg_v[:, 0:2, :])
            load_rows(1, w_pg_v[:, 2:4, :])
            for j in range(2):
                sp.dma_start(wide[:, 2 + j, 0:D], e_dram[j]).then_inc(e_in[j], DMA)
            sp.wait_ge(wd_lo, 2 * NCH)
            sp.dma_start(raw_b[:, 0, :], g_ple_post[0].partition_broadcast(P)).then_inc(gfin_in, DMA)
            sp.dma_start(raw_b[:, 1, :], g_final.partition_broadcast(P)).then_inc(gfin_in, DMA)
            sp.wait_ge(w_lo, GU0 + 4 * NCH + 4)
            load_rows(0, w_pg_v[:, 4:6, :])
            load_rows(1, w_pg_v[:, 6:8, :])
            for t in range(TT):
                if t + 2 < TT:
                    sp.wait_ge(ge_ok, t + 1)
                    sp.dma_start(wide[:, 2 + t % 2, 0:D], e_dram[t + 2]).then_inc(e_in[t % 2], DMA)
                sp.wait_ge(fin_ok, t + 1)
                sp.dma_start(out_v[t], scr[:, t % 2, :]).then_inc(out_stored[t % 2], DMA)
            for j in range(2):
                sp.wait_ge(out_stored[j], DMA * (TT // 2))

        @block.gpsimd
        def _(pool):
            def rms(n, ready, ms_done, done, k):
                pool.wait_ge(ready, k)
                pool.tensor_scalar(ss[:, n:n + 1], ss[:, n:n + 1], 1.0 / D, EPS, ALU.mult, ALU.add)\
                    .then_inc(ms_done, 1)
                pool.wait_ge(ms_done, k)
                pool.tensor_tensor(rs[:, n:n + 1], ss[:, n:n + 1], neg_half[:, :], ALU.pow).then_inc(done, 1)

            def lo(dst, src, hi, done):
                pool.tensor_tensor(dst, src, hi.bitcast(F32), ALU.subtract).then_inc(done, 1)

            def split_cols(m, n, hi=ws_hi, lo_=ws_lo, at=None):
                pool.wait_ge(w_hi, n)
                at = m if at is None else at
                lo(cols_stripe(lo_, at), cols_of(raw, m), cols_stripe(hi, at), w_lo)

            def split_row(src, r, dst_hi, dst_lo, n):
                pool.wait_ge(w_hi, n)
                lo(dst_lo, src[:, r, :], dst_hi, w_lo)

            pool.memset(ident[:, :], 0.0).then_inc(ident_ok, 1)
            pool.memset(neg_half[:, :], -0.5).then_inc(tables_ok, 1)
            pool.wait_ge(ident_ok, 1)
            pool.affine_select(out=ident[:, :], in_=ident[:, :], compare_op=ALU.not_equal, fill=1.0,
                               base=0, pattern=[[-1, P]], channel_multiplier=1).then_inc(ident_ok, 1)
            pool.wait_ge(tables_ok, 1)

            def norm_1(t):
                rms(t, ss_ok, ms_ok, rs_ok, t + 1)

            norm_1(0)
            norm_1(1)
            norm_1(2)
            norm_1(3)
            split_cols(0, 1)
            split_cols(1, 2)
            norm_1(4)
            norm_1(5)
            norm_1(6)
            norm_1(7)
            split_cols(2, 3)
            split_cols(3, 4)
            pool.wait_ge(xn_ok, TT)
            pool.memset(u_all[:, :, 0:PAD], 0.0).then_inc(upad_ok, 1)
            for g in range(GROUPS):
                for n in range(2 << g):
                    pool.memset(head[:, g, n:n + 1], (2 << g) / (n + 1)).then_inc(tables_ok, 1)
            pool.memset(wide[:, :, 0:HEADPAD], 0.0).then_inc(tables_ok, 1)
            pool.wait_ge(tables_ok, N_TABLES)

            def gate_u(n):
                h, c = AB[n]
                pool.wait_ge(ab_ev, n + 1)
                u = u_all[:, c, PAD + h * BANK:PAD + (h + 1) * BANK]
                pool.tensor_tensor(u, u, sigmoid_b(n), ALU.mult).then_inc(u_ok, 1)

            def sum_taps(j):
                pool.wait_ge(taps_in, j + 1)
                pool.tensor_tensor(gain[:, :], gain[:, :], scr[:, 2, :], ALU.add).then_inc(taps_sum, 1)

            def p_low(k):
                pool.wait_ge(p_copied, 2 * (k + 1))
                lo(bs_lo[:, k, :], wide[:, 1, HEADPAD:], bs_hi[:, k, :], p_lo_ok)

            gate_u(0)
            sum_taps(0)
            gate_u(1)
            pool.wait_ge(w_lo, S_B + 2)
            for m in range(2, 4):
                split_cols(m, S_B + m + 1, bs_hi, bs_lo)
            gate_u(2)
            sum_taps(1)
            gate_u(3)
            gate_u(4)
            p_low(0)
            sum_taps(2)
            gate_u(5)
            p_low(1)
            for r in range(KP):
                split_row(raw_b, r, bs_hi[:, 2 + r, :], bs_lo[:, 2 + r, :], S_PLE + r + 1)
            gate_u(6)
            sum_taps(3)
            for s in range(2):
                split_cols(V_STRIPE[s], S_V + s + 1, at=s)
            gate_u(7)
            for s in range(2, 4):
                split_cols(V_STRIPE[s], S_V + s + 1, at=s)

            steps = [0]

            def window(s, taps=None):
                g = V_GROUP[s]
                src = wide[:, 3 * (s % 2), :]
                pool.wait_ge(v_ev, s + 1)
                for j in range(g + 1):
                    dst, sh = wide[:, 1 + j % 2, :], 1 << j
                    if j:
                        pool.wait_ge(win_step, steps[0])
                    steps[0] += 1
                    pool.tensor_tensor(dst[:, HEADPAD:], src[:, HEADPAD:],
                                       src[:, HEADPAD - sh:HEADPAD + SEQ - sh], ALU.add).then_inc(win_step, 1)
                    src = dst
                    if taps is not None and j == 1:
                        sum_taps(taps)
                pool.wait_ge(win_step, steps[0])
                first = src[:, HEADPAD:HEADPAD + (2 << g)]
                pool.tensor_tensor(first, first, head[:, g, 0:2 << g], ALU.mult).then_inc(head_ok, 1)
                pool.wait_ge(head_ok, s + 1)
                pool.wait_ge(wv_ok, s + 1)
                pool.tensor_tensor(scr[:, s % 2, :], src[:, HEADPAD:], scr[:, s % 2, :], ALU.subtract)\
                    .then_inc(pooled_ok, 1)
                pool.wait_ge(pooled_ok, s + 1)

            def pooled_low(s):
                pool.wait_ge(pooled_hi, s + 1)
                lo(ws_lo[:, s, :], scr[:, s % 2, :], ws_hi[:, s, :], pooled_lo)

            def q_low(s):
                k = KC + V_GROUP[s]
                pool.wait_ge(q_copied, 2 * (s + 1))
                lo(act_lo[:, k, :], q_place(s), act_hi[:, k, :], q_lo_ok)

            def ln_rs(h):
                pool.wait_ge(var_ok, HT * (h + 1))
                for t in range(h * HT, (h + 1) * HT):
                    pool.tensor_tensor(lrs[:, t:t + 1], mv[:, t, 1:2], neg_half[:, :], ALU.pow).then_inc(lrs_ok, 1)

            def wo_q(j):
                split_row(raw, 3 - j, bs_hi[:, 3 - j, :], bs_lo[:, 3 - j, :], S_WOQ + j + 1)

            window(0, 4)
            ln_rs(0)
            window(1)
            pooled_low(0)
            sum_taps(5)
            window(2)
            pool.wait_ge(pw_hi_ok, 1)
            lo(act_lo[:, 2, BANK:2 * BANK], pw_raw[:, :], act_hi[:, 2, BANK:2 * BANK], pw_lo_ok)
            pooled_low(1)
            window(3)
            sum_taps(6)
            q_low(0)
            pooled_low(2)
            q_low(1)
            pooled_low(3)
            wo_q(0)
            q_low(2)
            sum_taps(7)
            wo_q(1)
            q_low(3)
            wo_q(2)
            wo_q(3)
            for j, k in enumerate((2, 3, 0, 1)):
                split_row(raw, k, ws_hi[:, k, :], ws_lo[:, k, :], S_WOU + j + 1)
            e_cols = slice(4 * TT, 5 * TT)
            pool.wait_ge(e_sq, TT)
            pool.tensor_scalar(ss[:, e_cols], ss[:, e_cols], 1.0 / D, EPS, ALU.mult, ALU.add).then_inc(e_ms, 1)
            pool.wait_ge(e_ms, 1)
            for t in range(TT):
                n = 4 * TT + t
                pool.tensor_tensor(rs[:, n:n + 1], ss[:, n:n + 1], neg_half[:, :], ALU.pow).then_inc(e_rs, 1)
            for t in range(4):
                rms(TT + t, ss_ok, ms_ok, rs_ok, TT + t + 1)
            ln_rs(1)
            for t in range(4, TT):
                rms(TT + t, ss_ok, ms_ok, rs_ok, TT + t + 1)
            for m in range(4):
                split_cols(m, GU0 + m + 1)

            def ffn_splits(i, last):
                for f in range(2):
                    pool.wait_ge(wd_hi, i * 2 + (f + 1))
                    lo(bs_lo[:, f, :], raw_b[:, f, :], bs_hi[:, f, :], wd_lo)
                for m in range(4):
                    if last:
                        split_row(raw, m, ws_hi[:, m, :], ws_lo[:, m, :], GU0 + 4 * NCH + m + 1)
                    else:
                        split_cols(m, i * 4 + (GU0 + 4 + m + 1))

            with pool.Fori(0, NCH - 1) as i:
                ffn_splits(i, False)
            ffn_splits(NCH - 1, True)

            def times_post(t):
                pool.wait_ge(e_in[t % 2], DMA * (t // 2 + 1))
                if t == 0:
                    pool.wait_ge(gfin_in, 2 * DMA)
                e = wide[:, 2 + t % 2, 0:D]
                pool.tensor_tensor(e, e, raw_b[:, 0, :], ALU.mult).then_inc(eg_ok, 1)

            for t in range(TT):
                rms(2 * TT + t, ss_ok, ms_ok, rs_ok, 2 * TT + t + 1)
                if t < 2:
                    times_post(t)
            for t in range(TT):
                rms(3 * TT + t, ss_ok, ms_ok, rs_ok, 3 * TT + t + 1)
                if t + 2 < TT:
                    times_post(t + 2)

        @block.scalar
        def _(act):
            def copy(dst, src, done, scale=1.0):
                act.activation(dst, src, ACT.Copy, scale=scale).then_inc(done, 1)

            def split_cols(m, raw_count, dst=ws_hi, at=None, signal=None):
                act.wait_ge((signal or raw_in)[m % 2], raw_count)
                copy(cols_stripe(dst, m if at is None else at), cols_of(raw, m), w_hi)

            def split_row(r, dst, raw_count):
                act.wait_ge(raw_in[r // 2], raw_count)
                copy(dst, raw[:, r, :], w_hi)

            def square(t, norm):
                n = norm * TT + t
                if n:
                    act.wait_ge(ss_ok, n)
                act.activation(junk[:, :], xres[:, t, :], ACT.Square, accum_out=ss[:, n:n + 1]).then_inc(ss_ok, 1)

            def turned_hi(t, norm):
                n = norm * TT + t
                for j in range(2):
                    act.wait_ge(turned, 2 * n + j + 1)
                    copy(act_hi[:, 4 * j:4 * j + 4, t * P:(t + 1) * P],
                         ps[:, turn_bank(norm, t) + j, :].rearrange("p (k s) -> p k s", k=4), act_hi_ok)

            def square_x(t):
                act.wait_ge(x_in[t], DMA)
                square(t, 0)

            def evac_ab(n):
                h, c = AB[n]
                b = 2 * (n % 2)
                act.wait_ge(ab_mm, n + 1)
                if n == 0:
                    act.wait_ge(upad_ok, 1)
                if n >= 2:
                    act.wait_ge(u_ok, n - 1)
                act.activation(u_all[:, c, PAD + h * BANK:PAD + (h + 1) * BANK], ps[:, b, :], ACT.Copy)
                act.activation(sigmoid_b(n), ps[:, b + 1, :], ACT.Sigmoid)\
                    .then_inc(ab_ev, 1)

            def first_taps(j):
                h, c = divmod(j, KC)
                if j:
                    act.wait_ge(taps_done, (j - 1) * OPS + 2)
                else:
                    act.wait_ge(const_ok, 3)
                    act.wait_ge(xn_ok, TT)
                act.wait_ge(u_ok, 2 * KC if h else c + 1)
                for k in range(OWN):
                    dst = gain if k < 2 else scr[:, 2, :]
                    ins = act.activation(dst[:, (k % 2) * BANK:(k % 2 + 1) * BANK],
                                         u_all[:, c, k + h * BANK:k + (h + 1) * BANK],
                                         ACT.Identity if k == 0 else ACT.Copy, scale=convw[:, c * 32 + k:c * 32 + k + 1],
                                         **({"bias": convb[:, c:c + 1]} if k == 0 else {}))
                ins.then_inc(taps_in, 1)

            def copy_p(k):
                act.wait_ge(p_turned, k + 1)
                if k:
                    act.wait_ge(p_lo_ok, k)
                act.activation(wide[:, 1, HEADPAD:], pair(6), ACT.Copy).then_inc(p_copied, 1)
                copy(bs_hi[:, k, :], pair(6), p_copied)

            square_x(0)
            square_x(1)
            turned_hi(0, 0)
            square_x(2)
            turned_hi(1, 0)
            square_x(3)
            turned_hi(2, 0)
            split_cols(0, DMA, signal=first_in)
            turned_hi(3, 0)
            split_cols(1, DMA, signal=first_in)
            square_x(4)
            square_x(5)
            turned_hi(4, 0)
            square_x(6)
            turned_hi(5, 0)
            square_x(7)
            split_cols(2, DMA)
            split_cols(3, DMA)
            evac_ab(0)
            turned_hi(6, 0)
            turned_hi(7, 0)
            split_cols(0, 2 * DMA, bs_hi)
            first_taps(0)
            split_cols(1, 2 * DMA, bs_hi)
            evac_ab(1)
            for m in range(2, 4):
                split_cols(m, 2 * DMA, bs_hi)
            evac_ab(2)
            first_taps(1)
            evac_ab(3)
            evac_ab(4)
            copy_p(0)
            first_taps(2)
            evac_ab(5)
            copy_p(1)
            act.wait_ge(rawb_in, 2 * DMA)
            for r in range(KP):
                copy(bs_hi[:, 2 + r, :], raw_b[:, r, :], w_hi)
            evac_ab(6)
            act.wait_ge(ab_mm, 7)
            for s in range(2):
                split_cols(V_STRIPE[s], 3 * DMA, at=s)
            first_taps(3)
            evac_ab(7)
            for s in range(2, 4):
                split_cols(V_STRIPE[s], 3 * DMA, at=s)

            def evac_v(s):
                act.wait_ge(v_mm, s + 1)
                if s >= 2:
                    act.wait_ge(pooled_ok, s - 1)
                else:
                    act.wait_ge(u_ok, 2 * KC)
                copy(wide[:, 3 * (s % 2), HEADPAD:], pair(2 * (s % 2)), v_ev)

            def window_v(s):
                act.wait_ge(v_ev, s + 1)
                if s >= 2:
                    act.wait_ge(pooled_lo, s - 1)
                copy(scr[:, s % 2, :], wide[:, 3 * (s % 2), HEADPAD:], wv_ok, scale=float(2 << V_GROUP[s]))

            def pooled_high(s):
                act.wait_ge(pooled_ok, s + 1)
                act.wait_ge(v_mm, s + 1)
                copy(ws_hi[:, s, :], scr[:, s % 2, :], pooled_hi)

            def scale_shift(n):
                h, c = divmod(n, KC)
                y, sig = silu_place(n)
                b = LN_BANK[c] if h else 6 + c % 2
                act.wait_ge(lnb_mm, n + 1)
                if n == KC:
                    act.wait_ge(q_lo_ok, GROUPS)
                act.activation(y, ps[:, b, :], ACT.Identity, bias=lnb[:, c:c + 1], scale=lng[:, c:c + 1])
                act.activation(sig, ps[:, b, :], ACT.Sigmoid, bias=lnb[:, c:c + 1],
                               scale=lng[:, c:c + 1]).then_inc(y_ok, 1)

            def evac_e(t):
                act.wait_ge(e_mm, t + 1)
                if t:
                    act.wait_ge(e_sq, t)
                act.activation(junk[:, :], pair(2 * (t % 2)), ACT.Square,
                               accum_out=ss[:, 4 * TT + t:4 * TT + t + 1]).then_inc(e_sq, 1)
                if t >= 2:
                    act.wait_ge(e_stored[t % 2], DMA * (t // 2))
                copy(raw_b[:, t % 2, :], pair(2 * (t % 2)), e_ok)

            def evac_q(s):
                g = V_GROUP[s]
                act.wait_ge(q_mm, s + 1)
                if s == 1:
                    act.wait_ge(q_lo_ok, 1)
                act.activation(q_place(s), pair(6), ACT.Copy, scale=qscale[:, g:g + 1]).then_inc(q_copied, 1)
                copy(act_hi[:, KC + g, :], pair(6), q_copied, scale=qscale[:, g:g + 1])

            def wo_q(j):
                if j == 0:
                    act.wait_ge(e_mm, TT)
                split_row(3 - j, bs_hi[:, 3 - j, :], 4 * DMA)

            evac_v(0)
            window_v(0)
            first_taps(4)
            evac_v(1)
            window_v(1)
            pooled_high(0)
            scale_shift(0)
            scale_shift(1)
            first_taps(5)
            evac_v(2)
            window_v(2)
            scale_shift(2)
            scale_shift(3)
            evac_v(3)
            act.wait_ge(pw_in, DMA)
            copy(act_hi[:, 2, BANK:2 * BANK], pw_raw[:, :], pw_hi_ok)
            evac_e(0)
            pooled_high(1)
            evac_e(1)
            window_v(3)
            evac_e(2)
            pooled_high(2)
            evac_e(3)
            evac_q(0)
            first_taps(6)
            evac_e(4)
            evac_e(5)
            pooled_high(3)
            evac_e(6)
            evac_q(1)
            evac_e(7)
            wo_q(0)
            evac_q(2)
            first_taps(7)
            wo_q(1)
            evac_q(3)
            wo_q(2)
            wo_q(3)
            for k in (2, 3, 0, 1):
                split_row(k, ws_hi[:, k, :], 5 * DMA)

            def square_after(t, norm, count):
                act.wait_ge(rows_added, count)
                square(t, norm)

            for t in range(HT):
                square_after(t, 1, 2 * (t + 1))
            for n in range(KC, 2 * KC):
                scale_shift(n)
            square_after(4, 1, 10)
            square_after(5, 1, 12)
            turned_hi(0, 1)
            turned_hi(1, 1)
            square_after(6, 1, 14)
            turned_hi(2, 1)
            turned_hi(3, 1)
            square_after(7, 1, 16)
            act.wait_ge(rows_done, 2 * TT)
            split_cols(0, 6 * DMA)
            turned_hi(4, 1)
            split_cols(1, 6 * DMA)
            turned_hi(5, 1)
            split_cols(2, 6 * DMA)
            split_cols(3, 6 * DMA)
            turned_hi(6, 1)
            turned_hi(7, 1)

            def ffn(i, last):
                for f in range(2):
                    act.wait_ge(rawb_in, i * DMA + 3 * DMA)
                    act.wait_ge(rows_done, i * 16 + 16)
                    copy(bs_hi[:, f, :], raw_b[:, f, :], wd_hi)
                for f in range(2):
                    for h in range(HALVES):
                        s = 2 * f + h
                        act.wait_ge(gu_mm, i * 4 + (s + 1))
                        act.activation(wide[:, 0, (s % 2) * BANK:(s % 2 + 1) * BANK], ps[:, 2 * (s % 2), :],
                                       ACT.Sigmoid).then_inc(sig_ok, 1)
                        act.wait_ge(in_ok, i * 4 + (s + 1))
                        copy(bs_hi[:, 2 + f, h * BANK:(h + 1) * BANK],
                             wide[:, 1, (s % 2) * BANK:(s % 2 + 1) * BANK], in_hi)
                    act.wait_ge(gu_mm, i * 4 + (2 * f + 2))
                    for m in (2 * f, 2 * f + 1):
                        if last:
                            split_row(m, ws_hi[:, m, :], (7 + NCH - 1) * DMA)
                        else:
                            split_cols(m, i * DMA + 7 * DMA)

            with act.Fori(0, NCH - 1) as i:
                ffn(i, False)
            ffn(NCH - 1, True)
            for t in range(TT):
                square_after(t, 2, 16 * NCH + 2 * (t + 1))
                if t >= 2:
                    turned_hi(t - 2, 2)
            act.wait_ge(rows_done, 16 * (NCH + 1))
            for k in range(4):
                act.wait_ge(raw_in[k // 2], (7 + NCH) * DMA)
                copy(bs_hi[:, k, :], raw[:, k, :], pg_hi)
            turned_hi(TT - 2, 2)

            def gate(t):
                act.wait_ge(pg_mm, t + 1)
                if t >= 2:
                    act.wait_ge(res_ok, t - 1)
                act.activation(wide[:, t % 2, 0:D], pair(PG_BANK[t % 3]), ACT.Sigmoid).then_inc(gate_ok, 1)

            gate(0)
            turned_hi(TT - 1, 2)
            for t in range(TT):
                if t:
                    gate(t)
                act.wait_ge(res_ok, t + 1)
                square(t, 3)

        @block.tensor
        def _(pe):
            def product(dst, w_hi_, w_lo_, m_hi, m_lo, start, stop):
                pe.matmul(dst, w_lo_, m_hi, start=start, stop=False)
                pe.matmul(dst, w_hi_, m_lo, start=False, stop=False)
                return pe.matmul(dst, w_hi_, m_hi, start=False, stop=stop)

            def cols_mm(bank, m, h, kk=range(KD), stripes=None):
                hi_, lo_ = stripes or (ws_hi, ws_lo)
                for k in kk:
                    w = slice(k * P, (k + 1) * P)
                    mv_ = slice(h * BANK, (h + 1) * BANK)
                    last = product(ps[:, bank, :], hi_[:, m, w], lo_[:, m, w],
                                   act_hi[:, k, mv_], act_lo[:, k, mv_], k == 0, k == KD - 1)
                return last

            def rows_mm(bank0, t, ks, stripes, first, final, rows=None):
                lasts = []
                for d in range(2):
                    for j, k in enumerate(ks):
                        hi_, lo_, r = stripes(k)
                        c = slice(d * BANK, (d + 1) * BANK)
                        r_hi, r_lo = rows or (act_hi, act_lo)
                        last = product(ps[:, bank0 + d, :], r_hi[:, k, t * P:(t + 1) * P],
                                       r_lo[:, k, t * P:(t + 1) * P], hi_[:, r, c], lo_[:, r, c],
                                       first and j == 0, final and j == len(ks) - 1)
                    lasts.append(last)
                return lasts

            def turn(t, norm, waits=()):
                n = norm * TT + t
                pe.wait_ge(xn_ok, n + 1)
                for j in range(2):
                    if norm == 0 and t >= 2:
                        pe.wait_ge(act_lo_ok, 2 * n + j - 3)
                    elif norm == 1 and t:
                        pe.wait_ge(act_lo_ok, 2 * n + j - 1)
                    elif norm == 2 and t >= 2:
                        pe.wait_ge(act_lo_ok, 2 * n + j - 3)
                    for q in range(4):
                        k = 4 * j + q
                        ins = pe.transpose(ps[:, turn_bank(norm, t) + j, q * P:(q + 1) * P],
                                           scr[:, n % 2, k * P:(k + 1) * P], ident[:, :])
                    ins.then_inc(turned, 1)

            pe.wait_ge(ident_ok, 2)
            for t in range(HT):
                turn(t, 0)

            def ab_part(n, j, kk=range(KD)):
                h, c = AB[n]
                hi_, lo_, m = ab_at(c)
                return cols_mm(2 * (n % 2) + j, m + j, h, kk, (hi_, lo_))

            pe.wait_ge(w_lo, 1)
            pe.wait_ge(act_lo_ok, 2 * HT)
            ab_part(0, 0)
            turn(4, 0)
            turn(5, 0)
            pe.wait_ge(const_in, 5 * DMA)
            for c in range(KC):
                pe.transpose(ps[:, 2, c * 32:c * 32 + TAPS], scr[0:TAPS, 2, c * P:(c + 1) * P],
                             ident[0:TAPS, 0:TAPS])
            pe.transpose(ps[:, 3, 0:4 * KC], scr[0:4 * KC, 2, C:C + P], ident[0:4 * KC, 0:4 * KC])\
              .then_inc(const_mm, 1)
            pe.wait_ge(w_lo, 2)
            ab_part(0, 1).then_inc(ab_mm, 1)
            turn(6, 0)
            turn(7, 0)
            for n in range(1, 2 * KC):
                h, c = AB[n]
                if h == 0:
                    pe.wait_ge(w_lo, 2 * c + 2)
                if n >= 2:
                    pe.wait_ge(ab_ev, n - 1)
                if n == 1:
                    pe.wait_ge(const_ok, 2)
                if n == KC:
                    pe.wait_ge(act_lo_ok, 2 * TT)
                ab_part(n, 0)
                ab_part(n, 1).then_inc(ab_mm, 1)
                if n in (4, 5):
                    k = n - 4
                    if k:
                        pe.wait_ge(p_copied, 2)
                    else:
                        pe.wait_ge(rawb_in, DMA)
                    for h in range(HALVES):
                        for q in range(HT):
                            ins = pe.transpose(ps[:, 6 + h, q * P:(q + 1) * P],
                                               raw_b[:, :, :].rearrange("p a (t d) -> p (a t) d", d=DP)
                                               [:, h * HT + q, k * P:(k + 1) * P], ident[:, :])
                    ins.then_inc(p_turned, 1)

            def conv_turn(t):
                for c in range(KC):
                    ins = pe.transpose(ps[:, LN_BANK[t % 4], c * P:(c + 1) * P],
                                       conv_o[:, c, t * P:(t + 1) * P], ident[:, :])
                ins.then_inc(lnf_mm, 1)

            def normed_turn(h, c):
                b = LN_BANK[c] if h else 6 + c % 2
                if h == 0 and c >= 2:
                    pe.wait_ge(y_ok, c - 1)
                for q in range(HT):
                    t = h * HT + q
                    ins = pe.transpose(ps[:, b, q * P:(q + 1) * P], conv_o[:, c, t * P:(t + 1) * P], ident[:, :])
                ins.then_inc(lnb_mm, 1)

            for s in range(GROUPS):
                pe.wait_ge(w_lo, S_V + s + 1)
                if s < 2:
                    pe.wait_ge(ab_ev, 2 * KC - 1 + s)
                else:
                    pe.wait_ge(v_ev, s - 1)
                cols_mm(2 * (s % 2), s, 0)
                cols_mm(2 * (s % 2) + 1, s, 1).then_inc(v_mm, 1)
                if s == 0:
                    pe.wait_ge(taps_done, KC * OPS)
                    pe.wait_ge(p_copied, 2 * KP)
                    for t in range(HT):
                        conv_turn(t)
                if s == 1:
                    pe.wait_ge(n_ok, HT)
                    normed_turn(0, 0)
                    normed_turn(0, 1)
                if s == 2:
                    normed_turn(0, 2)
                    normed_turn(0, 3)

            def q_group(s):
                g = V_GROUP[s]
                pe.wait_ge(pooled_lo, s + 1)
                if s:
                    pe.wait_ge(q_copied, 2 * s)
                else:
                    pe.wait_ge(y_ok, KC)
                    pe.wait_ge(pw_lo_ok, 1)
                w = slice(BANK + g * P, BANK + (g + 1) * P)
                for h in range(HALVES):
                    mv_ = slice(h * BANK, (h + 1) * BANK)
                    last = product(ps[:, 6 + h, :], act_hi[:, 2, w], act_lo[:, 2, w],
                                   ws_hi[:, s, mv_], ws_lo[:, s, mv_], True, True)
                last.then_inc(q_mm, 1)

            pe.wait_ge(p_lo_ok, KP)
            pe.wait_ge(w_lo, S_PLE + KP)
            for t in range(TT):
                if t < 2:
                    pe.wait_ge(v_ev, 3 + t)
                else:
                    pe.wait_ge(e_ok, t - 1)
                rows_mm(2 * (t % 2), t, range(KP), lambda k: (bs_hi, bs_lo, 2 + k), True, True,
                        (bs_hi, bs_lo))[-1].then_inc(e_mm, 1)
                if t == Q_AFTER[0]:
                    q_group(0)
                if t == Q_AFTER[1]:
                    q_group(1)
            q_group(2)
            q_group(3)

            def wo_stripe(k):
                return (bs_hi, bs_lo, k - 4) if k >= 4 else (ws_hi, ws_lo, k)

            def rows_out(t, ks, first, final):
                for ins in rows_mm(WO_BANK[t], t, ks, wo_stripe, first, final):
                    if final:
                        ins.then_inc(rows_done, 1)

            def pair_step(k, first, final):
                for t in range(2):
                    rows_out(t, (k,), first, final)

            pe.wait_ge(e_ok, TT)
            for j in range(4):
                pe.wait_ge(q_lo_ok, j + 1)
                pe.wait_ge(w_lo, S_WOQ + j + 1)
                pair_step(7 - j, j == 0, False)
            pe.wait_ge(mix_lo_ok, KC)
            for j, k in enumerate((2, 3, 0, 1)):
                pe.wait_ge(w_lo, S_WOU + j + 1)
                pair_step(k, False, j == 3)
            rows_out(2, (4, 5, 6, 7, 0, 1, 2, 3), True, True)
            pe.wait_ge(rows_added, 2)
            rows_out(3, (4, 5, 6, 7, 0, 1, 2, 3), True, True)
            pe.wait_ge(rows_added, 4)
            rows_out(4, (4, 5, 6, 7), True, False)
            pe.wait_ge(taps_done, 2 * OPS * KC)
            pe.wait_ge(rows_added, 6)
            for t in range(HT, TT):
                conv_turn(t)
            pe.wait_ge(rows_added, 8)
            rows_out(5, (4, 5, 6, 7), True, False)
            pe.wait_ge(n_ok, TT)
            for c in range(KC):
                normed_turn(1, c)
            pe.wait_ge(mix_lo_ok, 2 * KC)
            rows_out(4, range(4), False, True)
            rows_out(5, range(4), False, True)
            pe.wait_ge(y_ok, 2 * KC)
            turn(0, 1)
            turn(1, 1)
            pe.wait_ge(rows_added, 10)
            rows_out(6, (4, 5, 6, 7, 0, 1, 2, 3), True, True)
            turn(2, 1)
            turn(3, 1)
            pe.wait_ge(rows_added, 12)
            rows_out(7, (0, 1, 2, 3, 4, 5, 6, 7), True, True)
            turn(4, 1)
            turn(5, 1)
            pe.wait_ge(rows_added, 2 * TT)

            def down(i, t):
                h = t // HT
                if t % HT == 0:
                    pe.wait_ge(in_lo, i * 4 + (3 + h))
                for d in range(2):
                    n = 2 * t + d
                    pe.wait_ge(rows_added, i * 16 + (16 + n - 3))
                    for f in range(2):
                        last = product(ps[:, 4 + n % 4, :], bs_hi[:, 2 + f, t * P:(t + 1) * P],
                                       bs_lo[:, 2 + f, t * P:(t + 1) * P],
                                       bs_hi[:, f, d * BANK:(d + 1) * BANK], bs_lo[:, f, d * BANK:(d + 1) * BANK],
                                       f == 0, f == 1)
                    last.then_inc(rows_done, 1)

            def up_mm(f, h):
                cols_mm(2 * h, 2 * f, h)
                cols_mm(2 * h + 1, 2 * f + 1, h).then_inc(gu_mm, 1)

            def gate_up(i, f):
                pe.wait_ge(w_lo, i * 4 + (GU0 + 2 * f + 2))
                for h in range(HALVES):
                    if f:
                        pe.wait_ge(in_ok, i * 4 + (h + 1))
                    up_mm(f, h)

            pe.wait_ge(act_lo_ok, 2 * (TT + HT))
            pe.wait_ge(w_lo, GU0 + 1)
            cols_mm(0, 0, 0, range(4))
            turn(6, 1)
            cols_mm(0, 0, 0, range(4, 8))
            turn(7, 1)
            pe.wait_ge(w_lo, GU0 + 2)
            cols_mm(1, 1, 0).then_inc(gu_mm, 1)
            pe.wait_ge(act_lo_ok, 4 * TT)
            up_mm(0, 1)
            gate_up(0, 1)
            pe.wait_ge(wd_lo, 2)
            for t in range(TT):
                down(0, t)
            with pe.Fori(1, NCH - 1) as i:
                gate_up(i, 0)
                gate_up(i, 1)
                pe.wait_ge(wd_lo, i * 2 + 2)
                for t in range(TT):
                    down(i, t)
            gate_up(NCH - 1, 0)
            gate_up(NCH - 1, 1)
            pe.wait_ge(wd_lo, 2 * NCH)
            for t in range(TT):
                down(NCH - 1, t)
                if t == 2:
                    pe.wait_ge(in_lo, 4 * NCH)
                if t >= 2:
                    turn(t - 2, 2)

            def pg_stripe(k):
                return (ws_hi, ws_lo, k) if k < 4 else (bs_hi, bs_lo, k - 4)

            def gate_rows(t, ks):
                if ks[0] == 0:
                    pe.wait_ge(act_lo_ok, 2 * (2 * TT + t + 1))
                done = rows_mm(PG_BANK[t % 3], t, ks, pg_stripe, ks[0] == 0, ks[-1] == KD - 1)[-1]
                if ks[-1] == KD - 1:
                    done.then_inc(pg_mm, 1)

            pe.wait_ge(w_lo, GU0 + 4 * NCH + 4)
            pe.wait_ge(rows_added, 16 * (NCH + 1) - 2)
            gate_rows(0, range(4))
            turn(TT - 2, 2)
            pe.wait_ge(rows_added, 16 * (NCH + 1))
            gate_rows(1, range(4))
            turn(TT - 1, 2)
            pe.wait_ge(pg_lo, 4)
            gate_rows(0, range(4, 8))
            gate_rows(1, range(4, 8))
            for t in range(2, TT):
                if t == 2:
                    pe.wait_ge(act_lo_ok, 2 * 3 * TT)
                else:
                    pe.wait_ge(gate_ok, t - 2)
                gate_rows(t, range(8))

        @block.vector
        def _(dve):
            def lo(dst, src, hi, done):
                dve.tensor_tensor(dst, src, hi.bitcast(F32), ALU.subtract).then_inc(done, 1)

            def turned_lo(t, norm):
                n = norm * TT + t
                for j in range(2):
                    dve.wait_ge(act_hi_ok, 2 * n + j + 1)
                    at = (slice(None), slice(4 * j, 4 * j + 4), slice(t * P, (t + 1) * P))
                    lo(act_lo[at], ps[:, turn_bank(norm, t) + j, :].rearrange("p (k s) -> p k s", k=4),
                       act_hi[at], act_lo_ok)

            def normed(t, norm, gains):
                n = norm * TT + t
                if t == 0:
                    dve.wait_ge(gain_in, gains * DMA)
                dve.wait_ge(rs_ok, n + 1)
                if n >= 2:
                    dve.wait_ge(turned, 2 * n - 2)
                dve.scalar_tensor_tensor(out=scr[:, n % 2, :], in0=xres[:, t, :], scalar=rs[:, n:n + 1],
                                         in1=gain[:, :], op0=ALU.mult, op1=ALU.mult).then_inc(xn_ok, 1)

            normed(0, 0, 1)
            normed(1, 0, 1)
            for t in range(2, TT):
                turned_lo(t - 2, 0)
                normed(t, 0, 1)
            dve.wait_ge(const_mm, 1)
            dve.tensor_copy(convw[:, :].rearrange("p (c k) -> p c k", c=KC)[:, :, 0:TAPS],
                            ps[:, 2, 0:KC * 32].rearrange("p (c k) -> p c k", c=KC)[:, :, 0:TAPS])\
                .then_inc(const_ok, 1)
            dve.tensor_copy(cvec[:, :], ps[:, 3, 0:4 * KC]).then_inc(const_ok, 1)
            dve.wait_ge(const_ok, 2)
            for g in range(GROUPS):
                ins = dve.tensor_scalar(qscale[:, g:g + 1], pscale[:, g:g + 1], 1.0 / (2 << g), None, ALU.mult)
            ins.then_inc(const_ok, 1)
            turned_lo(TT - 2, 0)
            turned_lo(TT - 1, 0)

            for m in range(2):
                dve.wait_ge(w_hi, S_B + m + 1)
                dve.wait_ge(w_lo, S_B + m)
                lo(cols_stripe(bs_lo, m), cols_of(raw, m), cols_stripe(bs_hi, m), w_lo)

            even, odd = ps[:, 4, :], ps[:, 5, :]
            last_odd = TAPS - 1 if TAPS % 2 == 0 else TAPS - 2

            def convolve(c, h):
                done = h * KC * OPS
                conv_c = resid[:, bass.ds(c * SEQ + (KC * UW + h * BANK), BANK)]
                dve.wait_ge(taps_sum, c + (h * KC + 1))
                for n, k in enumerate(range(OWN, TAPS)):
                    acc = odd if k % 2 else even
                    if n >= 2:
                        dve.wait_ge(taps_done, c * OPS + (n - 1 + done))
                    dve.scalar_tensor_tensor(out=conv_c if k == last_odd else acc,
                                             in0=resid[:, bass.ds(c * UW + (k + h * BANK), BANK)],
                                             scalar=convw[:, bass.ds(c * 32 + k, 1)],
                                             in1=acc if n >= 2 else gain[:, (k % 2) * BANK:(k % 2 + 1) * BANK],
                                             op0=ALU.mult, op1=ALU.add).then_inc(taps_done, 1)
                dve.wait_ge(taps_done, c * OPS + (TAPS - OWN + done))
                dve.tensor_tensor(conv_c, even, conv_c, ALU.add).then_inc(taps_done, 1)
                dve.wait_ge(taps_done, c * OPS + (OPS + done))

            def layernorm(h):
                tiles = range(h * HT, (h + 1) * HT)
                for t in tiles:
                    dve.wait_ge(lnf_mm, t + 1)
                    dve.bn_stats(bst[:, t, :], ps[:, LN_BANK[t % 4], :]).then_inc(bn_ok, 1)
                for t in tiles:
                    dve.wait_ge(bn_ok, t + 1)
                    dve.bn_aggr(mv[:, t, :], bst[:, t, :]).then_inc(mv_ok, 1)
                for t in tiles:
                    dve.wait_ge(mv_ok, t + 1)
                    dve.tensor_scalar(mv[:, t, 1:2], mv[:, t, 1:2], EPS, None, ALU.add).then_inc(var_ok, 1)
                for t in tiles:
                    dve.wait_ge(lrs_ok, t + 1)
                    dve.tensor_scalar(conv_o[:, :, t * P:(t + 1) * P],
                                      ps[:, LN_BANK[t % 4], :].rearrange("p (c s) -> p c s", c=KC),
                                      mv[:, t, 0:1], lrs[:, t:t + 1], ALU.subtract, ALU.mult).then_inc(n_ok, 1)
                dve.wait_ge(n_ok, (h + 1) * HT)

            def silu(n):
                h, c = divmod(n, KC)
                y, sig = silu_place(n)
                at = (slice(None), c, slice(h * BANK, (h + 1) * BANK))
                dve.wait_ge(y_ok, n + 1)
                dve.tensor_tensor(y, y, sig, ALU.mult).then_inc(silu_ok, 1)
                dve.wait_ge(silu_ok, n + 1)
                dve.tensor_copy(act_hi[at], y).then_inc(mix_hi_ok, 1)
                dve.wait_ge(mix_hi_ok, n + 1)
                lo(act_lo[at], y, act_hi[at], mix_lo_ok)

            def add_x(t):
                dve.wait_ge(x_in[t], 2 * DMA)
                for d in range(2):
                    dve.wait_ge(rows_done, 2 * t + d + 1)
                    c = slice(d * BANK, (d + 1) * BANK)
                    dve.tensor_tensor(xres[:, t, c], ps[:, WO_BANK[t] + d, :], raw_b[:, t % 2, c], ALU.add)\
                       .then_inc(rows_added, 1)

            with dve.Fori(0, KC) as c:
                convolve(c, 0)
            layernorm(0)
            convolve(0, 1)
            dve.wait_ge(v_mm, GROUPS)
            for n in range(KC):
                silu(n)
            with dve.Fori(1, KC) as c:
                convolve(c, 1)
            add_x(0)
            add_x(1)
            add_x(2)
            add_x(3)
            layernorm(1)
            for n in range(KC, 2 * KC):
                silu(n)
            dve.wait_ge(mix_lo_ok, 2 * KC)
            normed(0, 1, 2)
            normed(1, 1, 2)
            add_x(4)
            add_x(5)
            turned_lo(0, 1)
            normed(2, 1, 2)
            turned_lo(1, 1)
            normed(3, 1, 2)
            add_x(6)
            turned_lo(2, 1)
            normed(4, 1, 2)
            turned_lo(3, 1)
            normed(5, 1, 2)
            add_x(7)
            turned_lo(4, 1)
            normed(6, 1, 2)
            turned_lo(5, 1)
            normed(7, 1, 2)
            turned_lo(6, 1)
            turned_lo(7, 1)

            def inner(i):
                for s in range(4):
                    f, h = divmod(s, 2)
                    a = slice((s % 2) * BANK, (s % 2 + 1) * BANK)
                    b = 2 * (s % 2)
                    dve.wait_ge(sig_ok, i * 4 + (s + 1))
                    dve.tensor_tensor(wide[:, 0, a], ps[:, b, :], wide[:, 0, a], ALU.mult).then_inc(gs_ok, 1)
                    dve.wait_ge(gs_ok, i * 4 + (s + 1))
                    if s >= 2:
                        dve.wait_ge(in_lo, i * 4 + (s - 1))
                    dve.tensor_tensor(wide[:, 1, a], wide[:, 0, a], ps[:, b + 1, :], ALU.mult).then_inc(in_ok, 1)
                    dve.wait_ge(in_hi, i * 4 + (s + 1))
                    at = (slice(None), 2 + f, slice(h * BANK, (h + 1) * BANK))
                    lo(bs_lo[at], wide[:, 1, a], bs_hi[at], in_lo)
                dve.wait_ge(in_lo, i * 4 + 4)

            def add_rows(i, t):
                for d in range(2):
                    n = 2 * t + d
                    dve.wait_ge(rows_done, i * 16 + (16 + n + 1))
                    x_ = xres[:, t, d * BANK:(d + 1) * BANK]
                    dve.tensor_tensor(x_, x_, ps[:, 4 + n % 4, :], ALU.add).then_inc(rows_added, 1)

            with dve.Fori(0, NCH - 1) as i:
                inner(i)
                for t in range(TT):
                    add_rows(i, t)
            inner(NCH - 1)
            for t in range(TT):
                add_rows(NCH - 1, t)
                if t:
                    normed(t - 1, 2, 3)
                if t >= 2:
                    turned_lo(t - 2, 2)
            normed(TT - 1, 2, 3)
            for k in range(4):
                dve.wait_ge(pg_hi, k + 1)
                lo(bs_lo[:, k, :], raw[:, k, :], bs_hi[:, k, :], pg_lo)
            turned_lo(TT - 2, 2)
            turned_lo(TT - 1, 2)

            def gated(t):
                g = wide[:, t % 2, 0:D]
                dve.wait_ge(gate_ok, t + 1)
                dve.wait_ge(eg_ok, t + 1)
                dve.scalar_tensor_tensor(out=g, in0=g, scalar=rs[:, 4 * TT + t:4 * TT + t + 1],
                                         in1=wide[:, 2 + t % 2, 0:D], op0=ALU.mult, op1=ALU.mult)\
                    .then_inc(ge_ok, 1)
                dve.wait_ge(ge_ok, t + 1)
                dve.tensor_tensor(xres[:, t, :], xres[:, t, :], g, ALU.add).then_inc(res_ok, 1)

            def final(t):
                dve.wait_ge(rs_ok, 3 * TT + t + 1)
                if t >= 2:
                    dve.wait_ge(out_stored[t % 2], DMA * (t // 2))
                dve.scalar_tensor_tensor(out=scr[:, t % 2, :], in0=xres[:, t, :],
                                         scalar=rs[:, 3 * TT + t:3 * TT + t + 1], in1=raw_b[:, 1, :],
                                         op0=ALU.mult, op1=ALU.mult).then_inc(fin_ok, 1)

            dve.wait_ge(gfin_in, 2 * DMA)
            dve.wait_ge(e_rs, TT)
            dve.wait_ge(turned, 2 * 3 * TT)
            for t in range(TT):
                gated(t)
                if t:
                    final(t - 1)
            final(TT - 1)


INPUTS = ["x", "p", "g_mix", "w_in", "conv_w", "conv_b", "ln_g", "ln_b", "pool_w", "pool_scale", "w_out",
          "g_ffn", "w_gate_up", "w_down", "g_ple_gate", "w_ple_gate", "w_ple_up", "g_ple_post", "g_final"]


def kernel(**inputs):
    import concourse.bacc as bacc
    from concourse.bass_utils import run_bass_kernel_spmd

    nc = bacc.Bacc("TRN2", target_bir_lowering=False, num_devices=1, dynamic_dma_scratch_size=1024)
    arrays, args = {}, {}
    for name in INPUTS:
        a = np.ascontiguousarray(inputs[name])
        arrays[f"in_{name}"] = a
        args[name] = nc.dram_tensor(f"in_{name}", a.shape, mybir.dt.from_np(a.dtype), kind="ExternalInput").ap()
    out = nc.dram_tensor("out_x", inputs["x"].shape, F32, kind="ExternalOutput").ap()
    hybrid_block(nc, out=out, **args)
    return run_bass_kernel_spmd(nc, [arrays], core_ids=[0]).results[0]["out_x"]
```

```python
from contextlib import ExitStack

import numpy as np

import concourse.bass as bass
from concourse import mybir

F32, F32R, BF16 = mybir.dt.float32, mybir.dt.float32r, mybir.dt.bfloat16
ALU, ACT = mybir.AluOpType, mybir.ActivationFunctionType

P = 128
EPS = 1e-6
BANK = 512
HEADPAD = 16
DMA = 16


def hybrid_block(nc, x, p, g_mix, w_in, conv_w, conv_b, ln_g, ln_b, pool_w, pool_scale, w_out,
                 g_ffn, w_gate_up, w_down, g_ple_gate, w_ple_gate, w_ple_up, g_ple_post,
                 g_final, out):
    SEQ, D = x.shape[1], x.shape[2]
    C = conv_w.shape[2]
    TAPS = conv_w.shape[1]
    GROUPS = pool_w.shape[1]
    F = w_down.shape[1]
    DP = p.shape[3]
    TT = SEQ // P
    KD = D // P
    KC = C // P
    KP = DP // P
    HALVES = SEQ // BANK
    HT = TT // HALVES
    NCH = F // (2 * P)
    PAD = TAPS - 1
    UW = PAD + SEQ
    assert (SEQ, D, C, KD, KC, KP, GROUPS, HALVES) == (1024, 1024, 512, 8, 4, 2, 4, 2)
    assert F == NCH * 2 * P

    x_v = x[0].rearrange("(t p) d -> t p d", p=P)
    out_v = out[0].rearrange("(t p) d -> t p d", p=P)
    p_v = p[0, 0].rearrange("(t p) d -> p t d", p=P)
    w_in_v = w_in[0].rearrange("(k p) n -> p k n", p=P)
    w_gu_v = w_gate_up[0].rearrange("(k p) n -> p k n", p=P)
    w_out_v = w_out[0].rearrange("(k p) n -> p k n", p=P)
    w_dn_v = w_down[0].rearrange("(f p) n -> p f n", p=P)
    w_pg_v = w_ple_gate[0].rearrange("(k p) n -> p k n", p=P)
    w_pu_v = w_ple_up[0].rearrange("(k p) n -> p k n", p=P)
    e_dram = nc.dram_tensor("e_scratch", (TT, P, D), F32, kind="Internal").ap()

    with ExitStack() as ctx:
        def sb(name, shape, dt=F32):
            return ctx.enter_context(nc.sbuf_tensor(name, shape, dt))

        def sem(name):
            return ctx.enter_context(nc.semaphore(name))

        resid = sb("resid", [P, KC * UW + KC * SEQ])
        xres = resid[:, 0:TT * D].rearrange("p (t d) -> p t d", t=TT)
        u_all = resid[:, 0:KC * UW].rearrange("p (c s) -> p c s", c=KC)
        conv_o = resid[:, KC * UW:KC * UW + KC * SEQ].rearrange("p (c s) -> p c s", c=KC)
        act_hi = sb("act_hi", [P, KD, SEQ], F32R)
        act_lo = sb("act_lo", [P, KD, SEQ], F32R)
        ws_hi = sb("ws_hi", [P, 4, 1024], F32R)
        ws_lo = sb("ws_lo", [P, 4, 1024], F32R)
        bs_hi = sb("bs_hi", [P, 4, 1024], F32R)
        bs_lo = sb("bs_lo", [P, 4, 1024], F32R)
        raw = sb("raw", [P, 4, 1024])
        raw_b = sb("raw_b", [P, 2, 1024])
        wide = sb("wide", [P, 4, SEQ + HEADPAD])
        scr = sb("scr", [P, 3, 1024])
        gain = sb("gain", [P, D])
        junk = sb("junk", [P, 1024], BF16)
        ident = sb("ident", [P, P])
        convw = sb("convw", [P, KC * 32])
        cvec = sb("cvec", [P, 4 * KC])
        qscale = sb("qscale", [P, GROUPS])
        convb, lng, lnb, pscale = (cvec[:, KC * n:KC * (n + 1)] for n in range(4))
        head = sb("head", [P, GROUPS, HEADPAD])
        pw_raw = sb("pw_raw", [P, GROUPS * P])
        neg_half = sb("neg_half", [P, 1])
        ss = sb("ss", [P, 5 * TT + 1])
        rs = sb("rs", [P, 5 * TT])
        bst = sb("bst", [P, TT, 6])
        mv = sb("mv", [P, TT, 2])
        lrs = sb("lrs", [P, TT])
        ps = ctx.enter_context(nc.psum_tensor("ps", [P, 8, BANK], F32))

        def cols_of(w, m):
            piece = w[:, 2 * (m % 2):2 * (m % 2) + 2, :].rearrange("p a (b n) -> p (a b) n", n=2 * P)
            return piece[:, :, (m // 2) * P:(m // 2 + 1) * P]

        def pair(b):
            return ps[:, b:b + 2, :].rearrange("p a b -> p (a b)")

        x_in = [sem(f"x_in{t}") for t in range(TT)]
        const_in = sem("const_in")
        gain_in = sem("gain_in")
        pw_in = sem("pw_in")
        first_in = [sem(f"first_in{j}") for j in range(2)]
        raw_in = [sem(f"raw_in{j}") for j in range(2)]
        rawb_in = sem("rawb_in")
        e_stored = [sem(f"e_stored{j}") for j in range(2)]
        e_in = [sem(f"e_in{t}") for t in range(TT)]
        gfin_in = sem("gfin_in")
        out_stored = [sem(f"out_stored{j}") for j in range(2)]
        ident_ok = sem("ident_ok")
        tables_ok = sem("tables_ok")
        upad_ok = sem("upad_ok")
        ss_ok = sem("ss_ok")
        ms_ok = sem("ms_ok")
        rs_ok = sem("rs_ok")
        xn_ok = sem("xn_ok")
        turned = sem("turned")
        act_hi_ok = sem("act_hi_ok")
        act_lo_ok = sem("act_lo_ok")
        w_hi = sem("w_hi")
        w_lo = sem("w_lo")
        wd_hi = sem("wd_hi")
        wd_lo = sem("wd_lo")
        ab_mm = sem("ab_mm")
        ab_ev = sem("ab_ev")
        u_ok = sem("u_ok")
        taps_in = sem("taps_in")
        taps_more = sem("taps_more")
        taps_sum = sem("taps_sum")
        taps_done = sem("taps_done")
        v_mm = sem("v_mm")
        v_ev = sem("v_ev")
        e_sq = sem("e_sq")
        e_ms = sem("e_ms")
        e_rs = sem("e_rs")
        wv_ok = sem("wv_ok")
        mix_hi_ok = sem("mix_hi_ok")
        win_step = sem("win_step")
        head_ok = sem("head_ok")
        pooled_ok = sem("pooled_ok")
        pooled_hi = sem("pooled_hi")
        pooled_lo = sem("pooled_lo")
        pw_hi_ok = sem("pw_hi_ok")
        pw_lo_ok = sem("pw_lo_ok")
        p_turned = sem("p_turned")
        p_copied = sem("p_copied")
        p_lo_ok = sem("p_lo_ok")
        e_mm = sem("e_mm")
        e_ok = sem("e_ok")
        q_mm = sem("q_mm")
        q_copied = sem("q_copied")
        q_lo_ok = sem("q_lo_ok")
        lnf_mm = sem("lnf_mm")
        bn_ok = sem("bn_ok")
        mv_ok = sem("mv_ok")
        var_ok = sem("var_ok")
        lrs_ok = sem("lrs_ok")
        n_ok = sem("n_ok")
        lnb_mm = sem("lnb_mm")
        y_ok = sem("y_ok")
        silu_ok = sem("silu_ok")
        mix_lo_ok = sem("mix_lo_ok")
        wo_used = sem("wo_used")
        const_mm = sem("const_mm")
        const_ok = sem("const_ok")
        rows_done = sem("rows_done")
        rows_added = sem("rows_added")
        gu_mm = sem("gu_mm")
        sig_ok = sem("sig_ok")
        gs_ok = sem("gs_ok")
        in_ok = sem("in_ok")
        in_hi = sem("in_hi")
        in_lo = sem("in_lo")
        pg_hi = sem("pg_hi")
        pg_lo = sem("pg_lo")
        pg_mm = sem("pg_mm")
        gate_ok = sem("gate_ok")
        eg_ok = sem("eg_ok")
        ge_ok = sem("ge_ok")
        res_ok = sem("res_ok")
        fin_ok = sem("fin_ok")

        N_IN, N_PLE, N_WO = 12, KP, KD
        N_TABLES = 2 + sum(2 << g for g in range(GROUPS))
        GU0 = N_IN + N_PLE + N_WO
        S_B, S_PLE, S_V, S_WOQ, S_WOU = 4, 8, 10, 14, 18
        V_STRIPE, V_GROUP = (2, 0, 3, 1), (3, 2, 1, 0)
        AB = [(0, c) for c in range(KC)] + [(1, c) for c in (2, 3, 0, 1)]
        PG_BANK = (4, 6, 2)
        WO_BANK = (0, 2, 6, 2, 6, 2, 6, 2)
        LN_BANK = ((6, 7, 4, 5), (4, 5, 0, 1))
        Q_AFTER = (3, 4, 5, 6)

        OWN = (6, 4)
        OPS = tuple(TAPS - n + 1 for n in OWN)
        TAPS_0, TAPS_ALL = KC * OPS[0], KC * sum(OPS)

        def ops_before(j):
            return min(j, KC) * OPS[0] + max(j - KC, 0) * OPS[1]

        def turn_bank(norm, t):
            return ((6, 4, 2, 0, 6, 4, 6, 4)[t], (0, 4, 0, 4, 0, 4, 6, 4)[t], 2 * (t % 2))[norm]

        def ab_at(c):
            return (ws_hi, ws_lo, 2 * c) if c < 2 else (bs_hi, bs_lo, 2 * (c - 2))

        def q_place(s):
            return wide[:, s, 0:SEQ]

        def sigmoid_b(n):
            return wide[:, 3, HEADPAD + (n % 2) * BANK:HEADPAD + (n % 2 + 1) * BANK]

        def silu_place(n):
            h, c = divmod(n, KC)
            if h:
                return wide[:, c, 0:BANK], wide[:, c, BANK:2 * BANK]
            return conv_o[:, c, 0:BANK], u_all[:, c, 0:BANK]

        def pieces(t):
            return (slice(0, D),) if t < TT - 1 else (slice(0, BANK), slice(BANK, D))

        def e_place(t):
            return raw[:, t - 2, :] if 2 <= t < TT - 2 else wide[:, 2 + t % 2, 0:D]

        def xn_place(n):
            return scr[:, (n - 2 * TT) % 3 if n >= 2 * TT else n % 2, :]

        def cols_stripe(w, m):
            return w[:, m, :].rearrange("p (k n) -> p k n", k=KD)

        block = ctx.enter_context(nc.Block())

        @block.sync
        def _(sp):
            def load_gain(g):
                sp.dma_start(gain[:, :], g.partition_broadcast(P)).then_inc(gain_in, DMA)

            def load_cols(view, lo, hi):
                for j, first in enumerate((lo, hi)):
                    sp.dma_start(raw[:, 2 * j:2 * j + 2, :].rearrange("p a (b n) -> p (a b) n", n=256),
                                 view[:, :, bass.ds(first, 256)]).then_inc(raw_in[j], DMA)

            def load_pair(half, signals):
                for j, first in enumerate((0, C)):
                    piece = raw[:, 2 * j:2 * j + 2, :].rearrange("p a (b n) -> p (a b) n", n=256)
                    sp.dma_start(piece[:, :, half * P:(half + 1) * P],
                                 w_in_v[:, :, first + half * P:first + (half + 1) * P]).then_inc(signals[j], DMA)

            def load_rows(j, rows):
                sp.dma_start(raw[:, 2 * j:2 * j + 2, :], rows).then_inc(raw_in[j], DMA)

            def load_x(t, dst):
                sp.dma_start(dst, x_v[t]).then_inc(x_in[t], DMA)

            load_x(0, xres[:, 0, :])
            load_gain(g_mix[0])
            for t in range(1, 4):
                load_x(t, xres[:, t, :])
            load_pair(0, first_in)
            load_pair(1, raw_in)
            sp.dma_start(scr[0:TAPS, 2, 0:C], conv_w[0]).then_inc(const_in, DMA)
            for n, src in enumerate((conv_b, ln_g, ln_b, pool_scale)):
                sp.dma_start(scr[KC * n:KC * (n + 1), 2, C:C + P], src[0].rearrange("(c p) -> c p", p=P))\
                  .then_inc(const_in, DMA)
            for t in range(4, TT):
                load_x(t, xres[:, t, :])
            sp.wait_ge(w_lo, S_B)
            load_cols(w_in_v, 256, C + 256)
            sp.dma_start(raw_b[:, :, :].rearrange("p a (t d) -> p (a t) d", d=DP), p_v).then_inc(rawb_in, DMA)
            sp.dma_start(pw_raw[:, :].rearrange("p (g d) -> p g d", g=GROUPS),
                         pool_w[0].rearrange("g c d -> c g d")).then_inc(pw_in, DMA)
            sp.wait_ge(w_lo, S_PLE)
            load_cols(w_in_v, 2 * C + 256, 2 * C)
            sp.wait_ge(p_turned, KP)
            sp.dma_start(raw_b[:, :, :], w_pu_v).then_inc(rawb_in, DMA)
            sp.wait_ge(w_lo, S_WOQ)
            load_rows(0, w_out_v[:, 4:6, :])
            load_rows(1, w_out_v[:, 6:8, :])
            for t in range(TT):
                sp.wait_ge(e_ok, t + 1)
                sp.dma_start(e_dram[t], raw_b[:, t % 2, :]).then_inc(e_stored[t % 2], DMA)
            sp.wait_ge(w_lo, S_WOQ + 2)
            load_rows(1, w_out_v[:, 2:4, :])
            sp.wait_ge(w_lo, S_WOQ + 4)
            load_rows(0, w_out_v[:, 0:2, :])
            for t in range(2):
                sp.wait_ge(e_stored[t], DMA * (TT // 2))
                load_x(t, raw_b[:, t, :])
            sp.wait_ge(taps_done, ops_before(2 * KC - 1) + 2)
            load_gain(g_ffn[0])
            sp.wait_ge(w_lo, GU0)
            load_cols(w_gu_v, 0, F)
            for t in range(2, TT):
                sp.wait_ge(rows_added, 2 * (t - 1))
                load_x(t, raw_b[:, t % 2, :])
            sp.wait_ge(rows_added, 2 * TT)
            sp.dma_start(raw_b[:, :, :], w_dn_v[:, 0:2, :]).then_inc(rawb_in, DMA)
            sp.wait_ge(xn_ok, 2 * TT)
            load_gain(g_ple_gate[0])
            with sp.Fori(0, NCH - 1) as i:
                sp.wait_ge(w_lo, i * 4 + (GU0 + 4))
                load_cols(w_gu_v, (i + 1) * 256, (i + 1) * 256 + F)
                sp.wait_ge(wd_lo, i * 2 + 2)
                sp.dma_start(raw_b[:, :, :], w_down[0][bass.ds((i + 1) * 256, 256), :]
                             .rearrange("(f p) n -> p f n", p=P)).then_inc(rawb_in, DMA)
            sp.wait_ge(w_lo, GU0 + 4 * NCH)
            load_rows(0, w_pg_v[:, 0:2, :])
            load_rows(1, w_pg_v[:, 2:4, :])
            def load_e(t):
                sp.dma_start(e_place(t), e_dram[t]).then_inc(e_in[t], DMA)

            load_e(0)
            load_e(1)
            sp.wait_ge(wd_lo, 2 * NCH)
            sp.dma_start(raw_b[:, 0, :], g_ple_post[0].partition_broadcast(P)).then_inc(gfin_in, DMA)
            sp.dma_start(raw_b[:, 1, :], g_final.partition_broadcast(P)).then_inc(gfin_in, DMA)
            sp.wait_ge(w_lo, GU0 + 4 * NCH + 4)
            load_rows(0, w_pg_v[:, 4:6, :])
            load_rows(1, w_pg_v[:, 6:8, :])
            sp.wait_ge(pg_lo, 4)
            for t in range(2, TT - 2):
                load_e(t)
            for t in range(2):
                sp.wait_ge(ge_ok, t + 1)
                load_e(TT - 2 + t)
            for t in range(TT):
                for j, c in enumerate(pieces(t)):
                    sp.wait_ge(fin_ok, t + j + 1)
                    sp.dma_start(out_v[t][:, c], scr[:, t % 2, c]).then_inc(out_stored[t % 2], DMA)
            sp.wait_ge(out_stored[0], DMA * (TT // 2))
            sp.wait_ge(out_stored[1], DMA * (TT // 2 + 1))

        @block.gpsimd
        def _(pool):
            def rms(n, ready, ms_done, done, k_ready, k=None):
                k = k or k_ready
                pool.wait_ge(ready, k_ready)
                pool.tensor_scalar(ss[:, n:n + 1], ss[:, n:n + 1], 1.0 / D, EPS, ALU.mult, ALU.add)\
                    .then_inc(ms_done, 1)
                pool.wait_ge(ms_done, k)
                pool.tensor_tensor(rs[:, n:n + 1], ss[:, n:n + 1], neg_half[:, :], ALU.pow).then_inc(done, 1)

            def lo(dst, src, hi, done):
                pool.tensor_tensor(dst, src, hi.bitcast(F32), ALU.subtract).then_inc(done, 1)

            def split_cols(m, n, hi=ws_hi, lo_=ws_lo, at=None):
                pool.wait_ge(w_hi, n)
                at = m if at is None else at
                lo(cols_stripe(lo_, at), cols_of(raw, m), cols_stripe(hi, at), w_lo)

            def split_row(src, r, dst_hi, dst_lo, n):
                pool.wait_ge(w_hi, n)
                lo(dst_lo, src[:, r, :], dst_hi, w_lo)

            pool.memset(ident[:, :], 0.0).then_inc(ident_ok, 1)
            pool.memset(neg_half[:, :], -0.5).then_inc(tables_ok, 1)
            pool.wait_ge(ident_ok, 1)
            pool.affine_select(out=ident[:, :], in_=ident[:, :], compare_op=ALU.not_equal, fill=1.0,
                               base=0, pattern=[[-1, P]], channel_multiplier=1).then_inc(ident_ok, 1)
            pool.wait_ge(tables_ok, 1)

            def norm_1(t):
                rms(t, ss_ok, ms_ok, rs_ok, t + 1)

            for t in range(4):
                norm_1(t)
            split_cols(0, 1)
            split_cols(1, 2)
            for t in range(4, TT):
                norm_1(t)
            pool.wait_ge(xn_ok, 4)
            pool.memset(u_all[:, :, 0:PAD], 0.0).then_inc(upad_ok, 1)
            for g in range(GROUPS):
                for n in range(2 << g):
                    pool.memset(head[:, g, n:n + 1], (2 << g) / (n + 1)).then_inc(tables_ok, 1)
            pool.memset(wide[:, :, 0:HEADPAD], 0.0).then_inc(tables_ok, 1)
            pool.wait_ge(tables_ok, N_TABLES)

            def gate_u(n):
                h, c = AB[n]
                pool.wait_ge(ab_ev, n + 1)
                u = u_all[:, c, PAD + h * BANK:PAD + (h + 1) * BANK]
                pool.tensor_tensor(u, u, sigmoid_b(n), ALU.mult).then_inc(u_ok, 1)

            def sum_taps(j):
                pool.wait_ge(taps_in, j + 1)
                if j < KC:
                    pool.tensor_tensor(scr[:, 2, :], scr[:, 2, :], wide[:, 0, HEADPAD:], ALU.add).then_inc(taps_more, 1)
                    pool.wait_ge(taps_more, j + 1)
                pool.tensor_tensor(gain[:, :], gain[:, :], scr[:, 2, :], ALU.add).then_inc(taps_sum, 1)

            def p_low(k):
                pool.wait_ge(p_copied, 2 * (k + 1))
                lo(bs_lo[:, k, :], wide[:, 1, HEADPAD:], bs_hi[:, k, :], p_lo_ok)

            gate_u(0)
            sum_taps(0)
            gate_u(1)
            pool.wait_ge(w_lo, S_B + 2)
            for m in range(2, 4):
                split_cols(m, S_B + m + 1, bs_hi, bs_lo)
            sum_taps(1)
            gate_u(2)
            gate_u(3)
            sum_taps(2)
            gate_u(4)
            p_low(0)
            sum_taps(3)
            gate_u(5)
            p_low(1)
            for r in range(KP):
                split_row(raw_b, r, bs_hi[:, 2 + r, :], bs_lo[:, 2 + r, :], S_PLE + r + 1)
            gate_u(6)
            for s in range(2):
                split_cols(V_STRIPE[s], S_V + s + 1, at=s)
            gate_u(7)
            for s in range(2, 4):
                split_cols(V_STRIPE[s], S_V + s + 1, at=s)

            steps = [0]

            def window(s):
                g = V_GROUP[s]
                src = wide[:, 3 * (s % 2), :]
                pool.wait_ge(v_ev, s + 1)
                for j in range(g + 1):
                    dst, sh = wide[:, 1 + j % 2, :], 1 << j
                    if j:
                        pool.wait_ge(win_step, steps[0])
                    steps[0] += 1
                    pool.tensor_tensor(dst[:, HEADPAD:], src[:, HEADPAD:],
                                       src[:, HEADPAD - sh:HEADPAD + SEQ - sh], ALU.add).then_inc(win_step, 1)
                    src = dst
                    if (s, j) == (0, 1):
                        ln_rs(0)
                        sum_taps(KC)
                pool.wait_ge(win_step, steps[0])
                first = src[:, HEADPAD:HEADPAD + (2 << g)]
                pool.tensor_tensor(first, first, head[:, g, 0:2 << g], ALU.mult).then_inc(head_ok, 1)
                pool.wait_ge(head_ok, s + 1)
                pool.wait_ge(wv_ok, s + 1)
                pool.tensor_tensor(scr[:, s % 2, :], src[:, HEADPAD:], scr[:, s % 2, :], ALU.subtract)\
                    .then_inc(pooled_ok, 1)
                pool.wait_ge(pooled_ok, s + 1)

            def pooled_low(s):
                pool.wait_ge(pooled_hi, s + 1)
                lo(ws_lo[:, s, :], scr[:, s % 2, :], ws_hi[:, s, :], pooled_lo)

            def q_low(s):
                k = KC + V_GROUP[s]
                pool.wait_ge(q_copied, 2 * (s + 1))
                lo(act_lo[:, k, :], q_place(s), act_hi[:, k, :], q_lo_ok)

            def ln_rs(h):
                pool.wait_ge(var_ok, HT * (h + 1))
                for t in range(h * HT, (h + 1) * HT):
                    pool.tensor_tensor(lrs[:, t:t + 1], mv[:, t, 1:2], neg_half[:, :], ALU.pow).then_inc(lrs_ok, 1)

            def wo_q(j):
                split_row(raw, 3 - j, ws_hi[:, j, :], ws_lo[:, j, :], S_WOQ + j + 1)

            window(0)
            sum_taps(5)
            window(1)
            pooled_low(0)
            pooled_low(1)
            window(2)
            pool.wait_ge(pw_hi_ok, 1)
            lo(act_lo[:, 2, BANK:2 * BANK], pw_raw[:, :], act_hi[:, 2, BANK:2 * BANK], pw_lo_ok)
            window(3)
            pooled_low(2)
            q_low(0)
            pooled_low(3)
            wo_q(0)
            q_low(1)
            wo_q(1)
            q_low(2)
            wo_q(2)
            q_low(3)
            wo_q(3)
            for j, k in enumerate((2, 3, 0, 1)):
                split_row(raw, k, bs_hi[:, k, :], bs_lo[:, k, :], S_WOU + j + 1)
            def norm_2(t):
                rms(TT + t, ss_ok, ms_ok, rs_ok, TT + t + 1)

            norm_2(0)
            norm_2(1)
            ln_rs(1)
            for t in range(2, TT - 1):
                norm_2(t)
            split_cols(0, GU0 + 1)
            split_cols(1, GU0 + 2)
            norm_2(TT - 1)
            split_cols(2, GU0 + 3)
            split_cols(3, GU0 + 4)

            def ffn_splits(i, last):
                for f in range(2):
                    pool.wait_ge(wd_hi, i * 2 + (f + 1))
                    lo(bs_lo[:, f, :], raw_b[:, f, :], bs_hi[:, f, :], wd_lo)
                for m in range(4):
                    if last:
                        split_row(raw, m, ws_hi[:, m, :], ws_lo[:, m, :], GU0 + 4 * NCH + m + 1)
                    else:
                        split_cols(m, i * 4 + (GU0 + 4 + m + 1))

            with pool.Fori(0, NCH - 1) as i:
                ffn_splits(i, False)
            ffn_splits(NCH - 1, True)

            def e_rms(t):
                rms(4 * TT + t, e_sq, e_ms, e_rs, t + 1)

            def times_post(t):
                pool.wait_ge(e_sq, t + 1)
                if t == 0:
                    pool.wait_ge(gfin_in, 2 * DMA)
                e = e_place(t)
                pool.tensor_tensor(e, e, raw_b[:, 0, :], ALU.mult).then_inc(eg_ok, 1)

            for t in range(TT):
                rms(2 * TT + t, ss_ok, ms_ok, rs_ok, 2 * TT + t + 1)
            for t in range(2):
                e_rms(t)
                times_post(t)
            for t in range(TT):
                if t == TT - 1:
                    pool.wait_ge(ss_ok, 3 * TT + t + 2)
                    n = 3 * TT + t
                    pool.tensor_tensor(ss[:, n:n + 1], ss[:, n:n + 1], ss[:, 5 * TT:5 * TT + 1], ALU.add)\
                        .then_inc(ss_ok, 1)
                rms(3 * TT + t, ss_ok, ms_ok, rs_ok, 3 * TT + t + (3 if t == TT - 1 else 1), 3 * TT + t + 1)
                if t + 2 < TT:
                    e_rms(t + 2)
                    times_post(t + 2)

        @block.scalar
        def _(act):
            def copy(dst, src, done, scale=1.0):
                act.activation(dst, src, ACT.Copy, scale=scale).then_inc(done, 1)

            def split_cols(m, raw_count, dst=ws_hi, at=None, signal=None):
                act.wait_ge((signal or raw_in)[m % 2], raw_count)
                copy(cols_stripe(dst, m if at is None else at), cols_of(raw, m), w_hi)

            def split_row(r, dst, raw_count):
                act.wait_ge(raw_in[r // 2], raw_count)
                copy(dst, raw[:, r, :], w_hi)

            def square(t, norm, c=slice(0, 1024), more=0):
                n = norm * TT + t
                at = 5 * TT if more else n
                if n:
                    act.wait_ge(ss_ok, n + more)
                act.activation(junk[:, c], xres[:, t, c], ACT.Square, accum_out=ss[:, at:at + 1]).then_inc(ss_ok, 1)

            def turned_hi(t, norm):
                n = norm * TT + t
                for j in range(2):
                    act.wait_ge(turned, 2 * n + j + 1)
                    copy(act_hi[:, 4 * j:4 * j + 4, t * P:(t + 1) * P],
                         ps[:, turn_bank(norm, t) + j, :].rearrange("p (k s) -> p k s", k=4), act_hi_ok)

            def square_x(t):
                act.wait_ge(x_in[t], DMA)
                square(t, 0)

            def evac_ab(n):
                h, c = AB[n]
                b = 2 * (n % 2)
                act.wait_ge(ab_mm, n + 1)
                if n == 0:
                    act.wait_ge(upad_ok, 1)
                if n >= 2:
                    act.wait_ge(u_ok, n - 1)
                act.activation(u_all[:, c, PAD + h * BANK:PAD + (h + 1) * BANK], ps[:, b, :], ACT.Copy)
                act.activation(sigmoid_b(n), ps[:, b + 1, :], ACT.Sigmoid)\
                    .then_inc(ab_ev, 1)

            def first_taps(j):
                h, c = divmod(j, KC)
                if j:
                    act.wait_ge(taps_done, ops_before(j - 1) + 2)
                else:
                    act.wait_ge(const_ok, 3)
                    act.wait_ge(xn_ok, TT)
                act.wait_ge(u_ok, 2 * KC if h else c + 1)
                for k in range(OWN[h]):
                    dst = (gain, scr[:, 2, :], wide[:, 0, HEADPAD:])[k // 2]
                    ins = act.activation(dst[:, (k % 2) * BANK:(k % 2 + 1) * BANK],
                                         u_all[:, c, k + h * BANK:k + (h + 1) * BANK],
                                         ACT.Identity if k == 0 else ACT.Copy, scale=convw[:, c * 32 + k:c * 32 + k + 1],
                                         **({"bias": convb[:, c:c + 1]} if k == 0 else {}))
                ins.then_inc(taps_in, 1)

            def copy_p(k):
                act.wait_ge(p_turned, k + 1)
                if k:
                    act.wait_ge(p_lo_ok, k)
                act.activation(wide[:, 1, HEADPAD:], pair(6), ACT.Copy).then_inc(p_copied, 1)
                copy(bs_hi[:, k, :], pair(6), p_copied)

            square_x(0)
            square_x(1)
            square_x(2)
            turned_hi(0, 0)
            square_x(3)
            turned_hi(1, 0)
            split_cols(0, DMA, signal=first_in)
            turned_hi(2, 0)
            turned_hi(3, 0)
            split_cols(1, DMA, signal=first_in)
            split_cols(2, DMA)
            split_cols(3, DMA)
            square_x(4)
            square_x(5)
            turned_hi(4, 0)
            turned_hi(5, 0)
            square_x(6)
            square_x(7)
            evac_ab(0)
            for m in range(2):
                split_cols(m, 2 * DMA, bs_hi)
            first_taps(0)
            turned_hi(6, 0)
            turned_hi(7, 0)
            evac_ab(1)
            for m in range(2, 4):
                split_cols(m, 2 * DMA, bs_hi)
            first_taps(1)
            evac_ab(2)
            evac_ab(3)
            first_taps(2)
            evac_ab(4)
            copy_p(0)
            first_taps(3)
            evac_ab(5)
            copy_p(1)
            act.wait_ge(rawb_in, 2 * DMA)
            for r in range(KP):
                copy(bs_hi[:, 2 + r, :], raw_b[:, r, :], w_hi)
            evac_ab(6)
            act.wait_ge(ab_mm, 7)
            for s in range(2):
                split_cols(V_STRIPE[s], 3 * DMA, at=s)
            evac_ab(7)
            for s in range(2, 4):
                split_cols(V_STRIPE[s], 3 * DMA, at=s)

            def evac_v(s):
                act.wait_ge(v_mm, s + 1)
                if s >= 2:
                    act.wait_ge(pooled_ok, s - 1)
                else:
                    act.wait_ge(u_ok, 2 * KC)
                copy(wide[:, 3 * (s % 2), HEADPAD:], pair(2 * (s % 2)), v_ev)

            def window_v(s):
                act.wait_ge(v_ev, s + 1)
                if s >= 2:
                    act.wait_ge(pooled_lo, s - 1)
                copy(scr[:, s % 2, :], wide[:, 3 * (s % 2), HEADPAD:], wv_ok, scale=float(2 << V_GROUP[s]))

            def pooled_high(s):
                act.wait_ge(pooled_ok, s + 1)
                act.wait_ge(v_mm, s + 1)
                copy(ws_hi[:, s, :], scr[:, s % 2, :], pooled_hi)

            def scale_shift(n):
                h, c = divmod(n, KC)
                y, sig = silu_place(n)
                b = LN_BANK[1][c] if h else 6 + c % 2
                act.wait_ge(lnb_mm, n + 1)
                if n == KC:
                    act.wait_ge(q_lo_ok, GROUPS)
                act.activation(y, ps[:, b, :], ACT.Identity, bias=lnb[:, c:c + 1], scale=lng[:, c:c + 1])
                act.activation(sig, ps[:, b, :], ACT.Sigmoid, bias=lnb[:, c:c + 1],
                               scale=lng[:, c:c + 1]).then_inc(y_ok, 1)

            def evac_e(t):
                act.wait_ge(e_mm, t + 1)
                if t >= 2:
                    act.wait_ge(e_stored[t % 2], DMA * (t // 2))
                copy(raw_b[:, t % 2, :], pair(2 * (t % 2)), e_ok)

            def evac_q(s):
                g = V_GROUP[s]
                act.wait_ge(q_mm, s + 1)
                act.activation(q_place(s), pair(6), ACT.Copy, scale=qscale[:, g:g + 1]).then_inc(q_copied, 1)
                copy(act_hi[:, KC + g, :], pair(6), q_copied, scale=qscale[:, g:g + 1])

            def wo_q(j):
                split_row(3 - j, ws_hi[:, j, :], 4 * DMA)

            evac_v(0)
            window_v(0)
            first_taps(4)
            first_taps(5)
            evac_v(1)
            window_v(1)
            pooled_high(0)
            scale_shift(0)
            scale_shift(1)
            evac_v(2)
            window_v(2)
            pooled_high(1)
            scale_shift(2)
            evac_v(3)
            scale_shift(3)
            window_v(3)
            act.wait_ge(pw_in, DMA)
            copy(act_hi[:, 2, BANK:2 * BANK], pw_raw[:, :], pw_hi_ok)
            evac_e(0)
            first_taps(6)
            evac_e(1)
            evac_e(2)
            pooled_high(2)
            evac_e(3)
            evac_q(0)
            pooled_high(3)
            evac_e(4)
            evac_q(1)
            wo_q(0)
            evac_e(5)
            evac_q(2)
            wo_q(1)
            evac_e(6)
            evac_q(3)
            evac_e(7)
            wo_q(2)
            first_taps(7)
            wo_q(3)
            act.wait_ge(e_mm, TT)
            for k in (2, 3, 0, 1):
                split_row(k, bs_hi[:, k, :], 5 * DMA)

            def square_after(t, norm, count):
                act.wait_ge(rows_added, count)
                square(t, norm)

            for t in range(4):
                square_after(t, 1, 2 * t + 2)
            for n in range(KC, 2 * KC):
                scale_shift(n)
            turned_hi(0, 1)
            turned_hi(1, 1)
            square_after(4, 1, 10)
            square_after(5, 1, 12)
            turned_hi(2, 1)
            turned_hi(3, 1)
            square_after(6, 1, 14)
            turned_hi(4, 1)
            turned_hi(5, 1)
            act.wait_ge(wo_used, 1)
            for m in range(4):
                split_cols(m, 6 * DMA)
            square_after(7, 1, 16)
            turned_hi(6, 1)
            turned_hi(7, 1)

            def ffn(i, last):
                for f in range(2):
                    act.wait_ge(rawb_in, i * DMA + 3 * DMA)
                    act.wait_ge(rows_done, i * 16 + 16)
                    copy(bs_hi[:, f, :], raw_b[:, f, :], wd_hi)
                for f in range(2):
                    for h in range(HALVES):
                        s = 2 * f + h
                        act.wait_ge(gu_mm, i * 4 + (s + 1))
                        act.activation(wide[:, 0, (s % 2) * BANK:(s % 2 + 1) * BANK], ps[:, 2 * (s % 2), :],
                                       ACT.Sigmoid).then_inc(sig_ok, 1)
                        act.wait_ge(in_ok, i * 4 + (s + 1))
                        copy(bs_hi[:, 2 + f, h * BANK:(h + 1) * BANK],
                             wide[:, 1, (s % 2) * BANK:(s % 2 + 1) * BANK], in_hi)
                    act.wait_ge(gu_mm, i * 4 + (2 * f + 2))
                    for m in (2 * f, 2 * f + 1):
                        if last:
                            split_row(m, ws_hi[:, m, :], (7 + NCH - 1) * DMA)
                        else:
                            split_cols(m, i * DMA + 7 * DMA)

            with act.Fori(0, NCH - 1) as i:
                ffn(i, False)
            ffn(NCH - 1, True)
            for t in range(TT):
                square_after(t, 2, 16 * NCH + 2 * (t + 1))
                if t >= 3:
                    turned_hi(t - 3, 2)
            act.wait_ge(rows_done, 16 * (NCH + 1))

            def pg_rows(ks):
                for k in ks:
                    act.wait_ge(raw_in[k // 2], (7 + NCH) * DMA)
                    copy(bs_hi[:, k, :], raw[:, k, :], pg_hi)

            pg_rows(range(4))
            turned_hi(TT - 3, 2)
            turned_hi(TT - 2, 2)

            def gate(t, j, c):
                act.wait_ge(pg_mm, t + j + 1)
                if t >= 2:
                    act.wait_ge(res_ok, t - 1)
                act.activation(wide[:, t % 2, c], pair(PG_BANK[t % 3])[:, c], ACT.Sigmoid).then_inc(gate_ok, 1)

            def square_e(t):
                act.wait_ge(e_in[t], DMA)
                if t:
                    act.wait_ge(e_sq, t)
                else:
                    act.wait_ge(ss_ok, 3 * TT)
                act.activation(junk[:, :], e_place(t), ACT.Square,
                               accum_out=ss[:, 4 * TT + t:4 * TT + t + 1]).then_inc(e_sq, 1)

            turned_hi(TT - 1, 2)
            square_e(0)
            square_e(1)
            for t in range(TT):
                for j, c in enumerate(pieces(t)):
                    gate(t, j, c)
                if t == 0:
                    act.wait_ge(e_sq, 2)
                for j, c in enumerate(pieces(t)):
                    act.wait_ge(res_ok, t + j + 1)
                    square(t, 3, c, j)
                if t + 2 < TT:
                    act.wait_ge(ss_ok, 3 * TT + t + 1)
                    square_e(t + 2)
                    act.wait_ge(e_sq, t + 3)
        @block.tensor
        def _(pe):
            def product(dst, w_hi_, w_lo_, m_hi, m_lo, start, stop):
                pe.matmul(dst, w_lo_, m_hi, start=start, stop=False)
                pe.matmul(dst, w_hi_, m_lo, start=False, stop=False)
                return pe.matmul(dst, w_hi_, m_hi, start=False, stop=stop)

            def cols_mm(bank, m, h, kk=range(KD), stripes=None):
                hi_, lo_ = stripes or (ws_hi, ws_lo)
                for k in kk:
                    w = slice(k * P, (k + 1) * P)
                    mv_ = slice(h * BANK, (h + 1) * BANK)
                    last = product(ps[:, bank, :], hi_[:, m, w], lo_[:, m, w],
                                   act_hi[:, k, mv_], act_lo[:, k, mv_], k == 0, k == KD - 1)
                return last

            def rows_mm(bank0, t, ks, stripes, first, final, rows=None):
                lasts = []
                for d in range(2):
                    for j, k in enumerate(ks):
                        hi_, lo_, r = stripes(k)
                        c = slice(d * BANK, (d + 1) * BANK)
                        r_hi, r_lo = rows or (act_hi, act_lo)
                        last = product(ps[:, bank0 + d, :], r_hi[:, k, t * P:(t + 1) * P],
                                       r_lo[:, k, t * P:(t + 1) * P], hi_[:, r, c], lo_[:, r, c],
                                       first and j == 0, final and j == len(ks) - 1)
                    lasts.append(last)
                return lasts

            def turn(t, norm):
                n = norm * TT + t
                pe.wait_ge(xn_ok, n + 1)
                for j in range(2):
                    if n >= 4 and t >= 2:
                        pe.wait_ge(act_lo_ok, 2 * n + j - 3)
                    for q in range(4):
                        k = 4 * j + q
                        ins = pe.transpose(ps[:, turn_bank(norm, t) + j, q * P:(q + 1) * P],
                                           xn_place(n)[:, k * P:(k + 1) * P], ident[:, :])
                    ins.then_inc(turned, 1)

            pe.wait_ge(ident_ok, 2)
            for t in range(HT):
                turn(t, 0)

            def ab_part(n, j, kk=range(KD)):
                h, c = AB[n]
                hi_, lo_, m = ab_at(c)
                return cols_mm(2 * (n % 2) + j, m + j, h, kk, (hi_, lo_))

            pe.wait_ge(w_lo, 1)
            pe.wait_ge(act_lo_ok, 2 * HT)
            ab_part(0, 0)
            turn(4, 0)
            turn(5, 0)
            pe.wait_ge(const_in, 5 * DMA)
            for c in range(KC):
                pe.transpose(ps[:, 2, c * 32:c * 32 + TAPS], scr[0:TAPS, 2, c * P:(c + 1) * P],
                             ident[0:TAPS, 0:TAPS])
            pe.transpose(ps[:, 3, 0:4 * KC], scr[0:4 * KC, 2, C:C + P], ident[0:4 * KC, 0:4 * KC])\
              .then_inc(const_mm, 1)
            pe.wait_ge(w_lo, 2)
            ab_part(0, 1).then_inc(ab_mm, 1)
            for n in range(1, 2 * KC):
                h, c = AB[n]
                if h == 0:
                    pe.wait_ge(w_lo, 2 * c + 2)
                if n >= 2:
                    pe.wait_ge(ab_ev, n - 1)
                if n == 1:
                    pe.wait_ge(const_ok, 2)
                if n == KC:
                    pe.wait_ge(act_lo_ok, 2 * TT)
                ab_part(n, 0)
                if n == 1:
                    turn(6, 0)
                    turn(7, 0)
                ab_part(n, 1).then_inc(ab_mm, 1)
                if n in (4, 5):
                    k = n - 4
                    if k:
                        pe.wait_ge(p_copied, 2)
                    else:
                        pe.wait_ge(rawb_in, DMA)
                    for h in range(HALVES):
                        for q in range(HT):
                            ins = pe.transpose(ps[:, 6 + h, q * P:(q + 1) * P],
                                               raw_b[:, :, :].rearrange("p a (t d) -> p (a t) d", d=DP)
                                               [:, h * HT + q, k * P:(k + 1) * P], ident[:, :])
                    ins.then_inc(p_turned, 1)

            def conv_turn(t):
                for c in range(KC):
                    ins = pe.transpose(ps[:, LN_BANK[t // HT][t % HT], c * P:(c + 1) * P],
                                       conv_o[:, c, t * P:(t + 1) * P], ident[:, :])
                ins.then_inc(lnf_mm, 1)

            def normed_turn(h, c):
                b = LN_BANK[1][c] if h else 6 + c % 2
                if h == 0 and c >= 2:
                    pe.wait_ge(y_ok, c - 1)
                for q in range(HT):
                    t = h * HT + q
                    ins = pe.transpose(ps[:, b, q * P:(q + 1) * P], conv_o[:, c, t * P:(t + 1) * P], ident[:, :])
                ins.then_inc(lnb_mm, 1)

            for s in range(GROUPS):
                pe.wait_ge(w_lo, S_V + s + 1)
                if s < 2:
                    pe.wait_ge(ab_ev, 2 * KC - 1 + s)
                else:
                    pe.wait_ge(v_ev, s - 1)
                cols_mm(2 * (s % 2), s, 0)
                cols_mm(2 * (s % 2) + 1, s, 1).then_inc(v_mm, 1)
                if s == 0:
                    pe.wait_ge(taps_done, TAPS_0)
                    pe.wait_ge(p_copied, 2 * KP)
                    for t in range(HT):
                        conv_turn(t)
                if s == 1:
                    pe.wait_ge(n_ok, HT)
                    normed_turn(0, 0)
                    normed_turn(0, 1)
                if s == 2:
                    normed_turn(0, 2)
                    normed_turn(0, 3)

            def q_group(s):
                g = V_GROUP[s]
                pe.wait_ge(pooled_lo, s + 1)
                if s:
                    pe.wait_ge(q_copied, 2 * s)
                else:
                    pe.wait_ge(y_ok, KC)
                    pe.wait_ge(pw_lo_ok, 1)
                w = slice(BANK + g * P, BANK + (g + 1) * P)
                for h in range(HALVES):
                    mv_ = slice(h * BANK, (h + 1) * BANK)
                    last = product(ps[:, 6 + h, :], act_hi[:, 2, w], act_lo[:, 2, w],
                                   ws_hi[:, s, mv_], ws_lo[:, s, mv_], True, True)
                last.then_inc(q_mm, 1)

            pe.wait_ge(p_lo_ok, KP)
            pe.wait_ge(w_lo, S_PLE + KP)
            for t in range(TT):
                if t < 2:
                    pe.wait_ge(v_ev, 3 + t)
                else:
                    pe.wait_ge(e_ok, t - 1)
                rows_mm(2 * (t % 2), t, range(KP), lambda k: (bs_hi, bs_lo, 2 + k), True, True,
                        (bs_hi, bs_lo))[-1].then_inc(e_mm, 1)
                if t in Q_AFTER:
                    q_group(Q_AFTER.index(t))

            def wo_stripe(k):
                return (ws_hi, ws_lo, KD - 1 - k) if k >= 4 else (bs_hi, bs_lo, k)

            def rows_out(t, ks, first, final):
                done = rows_mm(WO_BANK[t], t, ks, wo_stripe, first, final)
                if final:
                    for ins in done:
                        ins.then_inc(rows_done, 1)
                return done[-1]

            def pair_step(k, first, final):
                for t in range(2):
                    rows_out(t, (k,), first, final)

            pe.wait_ge(e_ok, TT)
            for j in range(4):
                pe.wait_ge(q_lo_ok, j + 1)
                pe.wait_ge(w_lo, S_WOQ + j + 1)
                pair_step(7 - j, j == 0, False)
            pe.wait_ge(mix_lo_ok, KC)
            for j, k in enumerate((2, 3, 0, 1)):
                pe.wait_ge(w_lo, S_WOU + j + 1)
                pair_step(k, False, j == 3)
            pe.wait_ge(q_copied, 2 * GROUPS)
            rows_out(2, range(KD), True, True)
            pe.wait_ge(taps_done, TAPS_ALL)
            conv_turn(4)
            conv_turn(5)
            pe.wait_ge(rows_added, 2)
            conv_turn(6)
            conv_turn(7)
            pe.wait_ge(rows_added, 4)
            rows_out(3, range(KD), True, True)
            pe.wait_ge(n_ok, TT)
            for c in range(KC):
                normed_turn(1, c)
            pe.wait_ge(rows_added, 6)
            rows_out(4, range(4, KD), True, False)
            pe.wait_ge(y_ok, 2 * KC)
            turn(0, 1)
            turn(1, 1)
            pe.wait_ge(rows_added, 8)
            rows_out(5, range(4, KD), True, False)
            pe.wait_ge(mix_lo_ok, 2 * KC)
            rows_out(4, range(4), False, True)
            rows_out(5, range(4), False, True)
            turn(2, 1)
            turn(3, 1)
            pe.wait_ge(rows_added, 10)
            rows_out(6, range(KD), True, True)
            turn(4, 1)
            turn(5, 1)
            pe.wait_ge(rows_added, 12)
            rows_out(7, range(4, KD), True, False).then_inc(wo_used, 1)
            rows_out(7, range(4), False, True)
            pe.wait_ge(rows_added, 14)
            turn(6, 1)

            def down(i, t):
                h = t // HT
                if t % HT == 0:
                    pe.wait_ge(in_lo, i * 4 + (3 + h))
                for d in range(2):
                    n = 2 * t + d
                    pe.wait_ge(rows_added, i * 16 + (16 + n - 3))
                    for f in range(2):
                        last = product(ps[:, 4 + n % 4, :], bs_hi[:, 2 + f, t * P:(t + 1) * P],
                                       bs_lo[:, 2 + f, t * P:(t + 1) * P],
                                       bs_hi[:, f, d * BANK:(d + 1) * BANK], bs_lo[:, f, d * BANK:(d + 1) * BANK],
                                       f == 0, f == 1)
                    last.then_inc(rows_done, 1)

            def up_mm(f, h):
                cols_mm(2 * h, 2 * f, h)
                cols_mm(2 * h + 1, 2 * f + 1, h).then_inc(gu_mm, 1)

            def gate_up(i, f):
                pe.wait_ge(w_lo, i * 4 + (GU0 + 2 * f + 2))
                for h in range(HALVES):
                    if f:
                        pe.wait_ge(in_ok, i * 4 + (h + 1))
                    up_mm(f, h)

            pe.wait_ge(act_lo_ok, 2 * (TT + HT))
            pe.wait_ge(w_lo, GU0 + 1)
            cols_mm(0, 0, 0)
            turn(7, 1)
            pe.wait_ge(w_lo, GU0 + 2)
            cols_mm(1, 1, 0).then_inc(gu_mm, 1)
            pe.wait_ge(rows_added, 2 * TT)
            pe.wait_ge(act_lo_ok, 4 * TT)
            up_mm(0, 1)
            gate_up(0, 1)
            pe.wait_ge(wd_lo, 2)
            for t in range(TT):
                down(0, t)
            with pe.Fori(1, NCH - 1) as i:
                gate_up(i, 0)
                gate_up(i, 1)
                pe.wait_ge(wd_lo, i * 2 + 2)
                for t in range(TT):
                    down(i, t)
            gate_up(NCH - 1, 0)
            gate_up(NCH - 1, 1)
            pe.wait_ge(wd_lo, 2 * NCH)
            for t in range(TT):
                down(NCH - 1, t)
                if t == 3:
                    pe.wait_ge(in_lo, 4 * NCH)
                if t >= 3:
                    turn(t - 3, 2)

            def pg_stripe(k):
                return (ws_hi, ws_lo, k) if k < 4 else (bs_hi, bs_lo, k - 4)

            def gate_rows(t, ks):
                if ks[0] == 0:
                    pe.wait_ge(act_lo_ok, 2 * (2 * TT + t + 1))
                done = rows_mm(PG_BANK[t % 3], t, ks, pg_stripe, ks[0] == 0, ks[-1] == KD - 1)
                if ks[-1] == KD - 1:
                    for ins in done[-len(pieces(t)):]:
                        ins.then_inc(pg_mm, 1)

            pe.wait_ge(w_lo, GU0 + 4 * NCH + 4)
            pe.wait_ge(rows_added, 16 * (NCH + 1) - 2)
            gate_rows(0, range(4))
            turn(TT - 3, 2)
            pe.wait_ge(rows_added, 16 * (NCH + 1))
            gate_rows(1, range(4))
            turn(TT - 2, 2)
            pe.wait_ge(pg_lo, 4)
            gate_rows(0, range(4, 8))
            turn(TT - 1, 2)
            gate_rows(1, range(4, 8))
            for t in range(2, TT):
                if t == 2:
                    pe.wait_ge(act_lo_ok, 2 * 3 * TT)
                else:
                    pe.wait_ge(gate_ok, t - 2)
                gate_rows(t, range(8))

        @block.vector
        def _(dve):
            def lo(dst, src, hi, done):
                dve.tensor_tensor(dst, src, hi.bitcast(F32), ALU.subtract).then_inc(done, 1)

            def turned_lo(t, norm):
                n = norm * TT + t
                for j in range(2):
                    dve.wait_ge(act_hi_ok, 2 * n + j + 1)
                    at = (slice(None), slice(4 * j, 4 * j + 4), slice(t * P, (t + 1) * P))
                    lo(act_lo[at], ps[:, turn_bank(norm, t) + j, :].rearrange("p (k s) -> p k s", k=4),
                       act_hi[at], act_lo_ok)

            def normed(t, norm, gains):
                n = norm * TT + t
                if t == 0:
                    dve.wait_ge(gain_in, gains * DMA)
                dve.wait_ge(rs_ok, n + 1)
                if n >= 2:
                    dve.wait_ge(turned, 2 * n - (4 if n >= 2 * TT + 3 else 2))
                dve.scalar_tensor_tensor(out=xn_place(n), in0=xres[:, t, :], scalar=rs[:, n:n + 1],
                                         in1=gain[:, :], op0=ALU.mult, op1=ALU.mult).then_inc(xn_ok, 1)

            normed(0, 0, 1)
            normed(1, 0, 1)
            normed(2, 0, 1)
            turned_lo(0, 0)
            normed(3, 0, 1)
            turned_lo(1, 0)
            turned_lo(2, 0)
            turned_lo(3, 0)
            for m in range(2, 4):
                dve.wait_ge(w_hi, m + 1)
                dve.wait_ge(w_lo, m)
                lo(cols_stripe(ws_lo, m), cols_of(raw, m), cols_stripe(ws_hi, m), w_lo)
            normed(4, 0, 1)
            normed(5, 0, 1)
            turned_lo(4, 0)
            turned_lo(5, 0)
            normed(6, 0, 1)
            normed(7, 0, 1)
            dve.wait_ge(const_mm, 1)
            dve.tensor_copy(convw[:, :].rearrange("p (c k) -> p c k", c=KC)[:, :, 0:TAPS],
                            ps[:, 2, 0:KC * 32].rearrange("p (c k) -> p c k", c=KC)[:, :, 0:TAPS])\
                .then_inc(const_ok, 1)
            dve.tensor_copy(cvec[:, :], ps[:, 3, 0:4 * KC]).then_inc(const_ok, 1)
            dve.wait_ge(const_ok, 2)
            for g in range(GROUPS):
                ins = dve.tensor_scalar(qscale[:, g:g + 1], pscale[:, g:g + 1], 1.0 / (2 << g), None, ALU.mult)
            ins.then_inc(const_ok, 1)
            for m in range(2):
                dve.wait_ge(w_hi, S_B + m + 1)
                lo(cols_stripe(bs_lo, m), cols_of(raw, m), cols_stripe(bs_hi, m), w_lo)
            turned_lo(6, 0)
            turned_lo(7, 0)
            dve.wait_ge(act_lo_ok, 2 * TT)

            even, odd = ps[:, 4, :], ps[:, 5, :]
            last_odd = TAPS - 1 if TAPS % 2 == 0 else TAPS - 2

            def convolve(c, h):
                own, ops, done = OWN[h], OPS[h], h * TAPS_0
                conv_c = resid[:, bass.ds(c * SEQ + (KC * UW + h * BANK), BANK)]
                dve.wait_ge(taps_sum, c + (h * KC + 1))
                for n, k in enumerate(range(own, TAPS)):
                    acc = odd if k % 2 else even
                    if n >= 2:
                        dve.wait_ge(taps_done, c * ops + (n - 1 + done))
                    dve.scalar_tensor_tensor(out=conv_c if k == last_odd else acc,
                                             in0=resid[:, bass.ds(c * UW + (k + h * BANK), BANK)],
                                             scalar=convw[:, bass.ds(c * 32 + k, 1)],
                                             in1=acc if n >= 2 else gain[:, (k % 2) * BANK:(k % 2 + 1) * BANK],
                                             op0=ALU.mult, op1=ALU.add).then_inc(taps_done, 1)
                dve.wait_ge(taps_done, c * ops + (TAPS - own + done))
                dve.tensor_tensor(conv_c, even, conv_c, ALU.add).then_inc(taps_done, 1)
                dve.wait_ge(taps_done, c * ops + (ops + done))

            def layernorm(h):
                tiles = range(h * HT, (h + 1) * HT)
                for t in tiles:
                    dve.wait_ge(lnf_mm, t + 1)
                    dve.bn_stats(bst[:, t, :], ps[:, LN_BANK[t // HT][t % HT], :]).then_inc(bn_ok, 1)
                for t in tiles:
                    dve.wait_ge(bn_ok, t + 1)
                    dve.bn_aggr(mv[:, t, :], bst[:, t, :]).then_inc(mv_ok, 1)
                for t in tiles:
                    dve.wait_ge(mv_ok, t + 1)
                    dve.tensor_scalar(mv[:, t, 1:2], mv[:, t, 1:2], EPS, None, ALU.add).then_inc(var_ok, 1)
                for t in tiles:
                    dve.wait_ge(lrs_ok, t + 1)
                    dve.tensor_scalar(conv_o[:, :, t * P:(t + 1) * P],
                                      ps[:, LN_BANK[t // HT][t % HT], :].rearrange("p (c s) -> p c s", c=KC),
                                      mv[:, t, 0:1], lrs[:, t:t + 1], ALU.subtract, ALU.mult).then_inc(n_ok, 1)
                dve.wait_ge(n_ok, (h + 1) * HT)

            def silu(n):
                h, c = divmod(n, KC)
                y, sig = silu_place(n)
                at = (slice(None), c, slice(h * BANK, (h + 1) * BANK))
                dve.wait_ge(y_ok, n + 1)
                dve.tensor_tensor(y, y, sig, ALU.mult).then_inc(silu_ok, 1)
                dve.wait_ge(silu_ok, n + 1)
                dve.tensor_copy(act_hi[at], y).then_inc(mix_hi_ok, 1)
                dve.wait_ge(mix_hi_ok, n + 1)
                lo(act_lo[at], y, act_hi[at], mix_lo_ok)

            def add_x(t):
                dve.wait_ge(x_in[t], 2 * DMA)
                for d in range(2):
                    dve.wait_ge(rows_done, 2 * t + d + 1)
                    c = slice(d * BANK, (d + 1) * BANK)
                    dve.tensor_tensor(xres[:, t, c], ps[:, WO_BANK[t] + d, :], raw_b[:, t % 2, c], ALU.add)\
                       .then_inc(rows_added, 1)

            with dve.Fori(0, KC) as c:
                convolve(c, 0)
            layernorm(0)
            with dve.Fori(0, 2) as c:
                convolve(c, 1)
            dve.wait_ge(v_mm, GROUPS)
            for n in range(KC):
                silu(n)
            with dve.Fori(2, KC) as c:
                dve.wait_ge(taps_in, c + (KC + 1))
                dve.tensor_tensor(gain[:, :], gain[:, :], scr[:, 2, :], ALU.add).then_inc(taps_sum, 1)
                convolve(c, 1)
            add_x(0)
            add_x(1)
            layernorm(1)
            add_x(2)
            normed(0, 1, 2)
            normed(1, 1, 2)
            add_x(3)
            for n in range(KC, 2 * KC):
                silu(n)
            turned_lo(0, 1)
            normed(2, 1, 2)
            turned_lo(1, 1)
            normed(3, 1, 2)
            add_x(4)
            add_x(5)
            for t in range(4, 6):
                turned_lo(t - 2, 1)
                normed(t, 1, 2)
            add_x(6)
            turned_lo(4, 1)
            normed(6, 1, 2)
            turned_lo(5, 1)
            add_x(7)
            turned_lo(6, 1)
            normed(7, 1, 2)
            turned_lo(7, 1)

            def inner(i):
                for s in range(4):
                    f, h = divmod(s, 2)
                    a = slice((s % 2) * BANK, (s % 2 + 1) * BANK)
                    b = 2 * (s % 2)
                    dve.wait_ge(sig_ok, i * 4 + (s + 1))
                    dve.tensor_tensor(wide[:, 0, a], ps[:, b, :], wide[:, 0, a], ALU.mult).then_inc(gs_ok, 1)
                    dve.wait_ge(gs_ok, i * 4 + (s + 1))
                    if s >= 2:
                        dve.wait_ge(in_lo, i * 4 + (s - 1))
                    dve.tensor_tensor(wide[:, 1, a], wide[:, 0, a], ps[:, b + 1, :], ALU.mult).then_inc(in_ok, 1)
                    dve.wait_ge(in_hi, i * 4 + (s + 1))
                    at = (slice(None), 2 + f, slice(h * BANK, (h + 1) * BANK))
                    lo(bs_lo[at], wide[:, 1, a], bs_hi[at], in_lo)
                dve.wait_ge(in_lo, i * 4 + 4)

            def add_rows(i, t):
                for d in range(2):
                    n = 2 * t + d
                    dve.wait_ge(rows_done, i * 16 + (16 + n + 1))
                    x_ = xres[:, t, d * BANK:(d + 1) * BANK]
                    dve.tensor_tensor(x_, x_, ps[:, 4 + n % 4, :], ALU.add).then_inc(rows_added, 1)

            with dve.Fori(0, NCH - 1) as i:
                inner(i)
                for t in range(TT):
                    add_rows(i, t)
            inner(NCH - 1)
            for t in range(TT):
                add_rows(NCH - 1, t)
                if t:
                    normed(t - 1, 2, 3)
                if t >= 3:
                    turned_lo(t - 3, 2)
            normed(TT - 1, 2, 3)

            def pg_rows(ks):
                for k in ks:
                    dve.wait_ge(pg_hi, k + 1)
                    lo(bs_lo[:, k, :], raw[:, k, :], bs_hi[:, k, :], pg_lo)

            pg_rows(range(4))
            turned_lo(TT - 3, 2)
            turned_lo(TT - 2, 2)
            turned_lo(TT - 1, 2)

            def gated(t, j, c):
                g = wide[:, t % 2, c]
                dve.wait_ge(gate_ok, t + j + 1)
                dve.wait_ge(eg_ok, t + 1)
                dve.wait_ge(e_rs, t + 1)
                dve.scalar_tensor_tensor(out=g, in0=g, scalar=rs[:, 4 * TT + t:4 * TT + t + 1],
                                         in1=e_place(t)[:, c], op0=ALU.mult, op1=ALU.mult)\
                    .then_inc(ge_ok, 1)
                dve.wait_ge(ge_ok, t + j + 1)
                dve.tensor_tensor(xres[:, t, c], xres[:, t, c], g, ALU.add).then_inc(res_ok, 1)

            def final(t):
                dve.wait_ge(rs_ok, 3 * TT + t + 1)
                if t >= 2:
                    dve.wait_ge(out_stored[t % 2], DMA * (t // 2))
                for c in pieces(t):
                    dve.scalar_tensor_tensor(out=scr[:, t % 2, c], in0=xres[:, t, c],
                                             scalar=rs[:, 3 * TT + t:3 * TT + t + 1], in1=raw_b[:, 1, c],
                                             op0=ALU.mult, op1=ALU.mult).then_inc(fin_ok, 1)

            dve.wait_ge(gfin_in, 2 * DMA)
            dve.wait_ge(turned, 2 * 3 * TT)
            for t in range(TT):
                for j, c in enumerate(pieces(t)):
                    gated(t, j, c)
                    if t and j == 0:
                        final(t - 1)
            final(TT - 1)


INPUTS = ["x", "p", "g_mix", "w_in", "conv_w", "conv_b", "ln_g", "ln_b", "pool_w", "pool_scale", "w_out",
          "g_ffn", "w_gate_up", "w_down", "g_ple_gate", "w_ple_gate", "w_ple_up", "g_ple_post", "g_final"]


def kernel(**inputs):
    import concourse.bacc as bacc
    from concourse.bass_utils import run_bass_kernel_spmd

    nc = bacc.Bacc("TRN2", target_bir_lowering=False, num_devices=1, dynamic_dma_scratch_size=1024)
    arrays, args = {}, {}
    for name in INPUTS:
        a = np.ascontiguousarray(inputs[name])
        arrays[f"in_{name}"] = a
        args[name] = nc.dram_tensor(f"in_{name}", a.shape, mybir.dt.from_np(a.dtype), kind="ExternalInput").ap()
    out = nc.dram_tensor("out_x", inputs["x"].shape, F32, kind="ExternalOutput").ap()
    hybrid_block(nc, out=out, **args)
    return run_bass_kernel_spmd(nc, [arrays], core_ids=[0]).results[0]["out_x"]
```
